# Optimizing a Trainium2 kernel written in Bass

```python
import math
import jax, jax.numpy as jnp
from jax import lax
import numpy as np
import jax
import jax.numpy as jnp

D_MODEL = 1024
BATCH = 1
SEQ = 256
DEPTH = 1

HEAD_DIM = 64
ATT_HEADS = 8
ATT_WIDTH = ATT_HEADS * HEAD_DIM
RWKV_HEADS = 8
RWKV_WIDTH = RWKV_HEADS * HEAD_DIM
MIX_WIDTH = ATT_WIDTH + RWKV_WIDTH
D_FF = 2816
N_DIRS = 2
DECAY_LORA = 64
ICLR_LORA = 64
GATE_LORA = 128
DILATED_PATTERNS = ((128, 1), (512, 4), (2048, 16))
ROPE_THETA = 10000.0
NORM_EPS = 1e-6
GN_EPS = 64e-5
ATT_IN = 3 * ATT_WIDTH
RWKV_IN = 3 * RWKV_WIDTH + N_DIRS * DECAY_LORA + N_DIRS * ICLR_LORA + GATE_LORA
IN_WIDTH = ATT_IN + RWKV_IN


def _rmsnorm(x, g):
    xf = x.astype(jnp.float32)
    return xf * lax.rsqrt(jnp.mean(xf * xf, axis=-1, keepdims=True) + NORM_EPS) * g.astype(jnp.float32)

def _swiglu(h, w_gate, w_up, w_down):
    return (jax.nn.silu(h @ w_gate) * (h @ w_up)) @ w_down

def _rope(t, cos, sin):
    half = t.shape[-1] // 2
    t1, t2 = t[..., :half], t[..., half:]
    c, s = cos[None, :, None, :], sin[None, :, None, :]
    return jnp.concatenate([t1 * c - t2 * s, t2 * c + t1 * s], axis=-1)

def _dilated_attention(q, k, v, window, dilation):
    B, S, H, Dh = q.shape
    L = S // dilation
    W = window // (2 * dilation)
    nb = -(-L // W)
    Lp = nb * W
    pad = Lp - L

    def to_sub(t):
        return t.reshape(B, L, dilation, H, Dh).transpose(0, 3, 2, 1, 4)

    qb = jnp.pad(to_sub(q), ((0, 0), (0, 0), (0, 0), (0, pad), (0, 0))).reshape(B, H, dilation, nb, W, Dh)

    def band(t):
        tp = jnp.pad(to_sub(t), ((0, 0), (0, 0), (0, 0), (W, W + pad), (0, 0))).reshape(B, H, dilation, nb + 2, W, Dh)
        return jnp.concatenate([tp[:, :, :, :-2], tp[:, :, :, 1:-1], tp[:, :, :, 2:]], axis=4)

    kb, vb = band(k), band(v)
    blk = jnp.arange(nb)[:, None, None] * W
    qi = blk + jnp.arange(W)[None, :, None]
    ki = blk - W + jnp.arange(3 * W)[None, None, :]
    valid = (jnp.abs(ki - qi) <= W) & (ki >= 0) & (ki < L)

    s = jnp.einsum('bhrnqd,bhrnkd->bhrnqk', qb, kb).astype(jnp.float32)
    s = jnp.where(valid, s, -jnp.inf)
    m = jnp.max(s, axis=-1, keepdims=True)
    p = jnp.exp(s - m)
    den = jnp.sum(p, axis=-1, keepdims=True)
    o = jnp.einsum('bhrnqk,bhrnkd->bhrnqd', p, vb.astype(jnp.float32)) / den
    lse = (m + jnp.log(den))[..., 0]
    o = o.reshape(B, H, dilation, Lp, Dh)[:, :, :, :L].transpose(0, 3, 2, 1, 4).reshape(B, S, H, Dh)
    lse = lse.reshape(B, H, dilation, Lp)[:, :, :, :L].transpose(0, 3, 2, 1).reshape(B, S, H)
    return o, lse

def _attention_group(za, cos, sin, out_g):
    B, S, _ = za.shape
    q, k, v = jnp.split(za, 3, axis=-1)
    q = _rope(q.reshape(B, S, ATT_HEADS, HEAD_DIM), cos, sin) * (HEAD_DIM ** -0.5)
    k = _rope(k.reshape(B, S, ATT_HEADS, HEAD_DIM), cos, sin)
    v = v.reshape(B, S, ATT_HEADS, HEAD_DIM)
    outs, lses = [], []
    for window, dilation in DILATED_PATTERNS:
        o, l = _dilated_attention(q, k, v, window, dilation)
        outs.append(o)
        lses.append(l)
    wts = jax.nn.softmax(jnp.stack(lses, axis=0), axis=0)
    o = jnp.sum(wts[..., None] * jnp.stack(outs, axis=0), axis=0)
    o = o * lax.rsqrt(jnp.mean(o * o, axis=-1, keepdims=True) + NORM_EPS)
    return o.reshape(B, S, ATT_WIDTH) * out_g

def _rwkv7_step(state, inp):
    r, w, k, v, kk, kka = inp
    sa = jnp.einsum('dbhvk,dbhk->dbhv', state, kk)
    state = state * w[..., None, :] - sa[..., :, None] * kka[..., None, :] + v[..., :, None] * k[..., None, :]
    y = jnp.einsum('dbhvk,dbhk->dbhv', state, r)
    return state, y

def _rwkv7_group(u, mu_prev, mu_next, w0, w2, a0, a2, g2, k_k, k_a, r_k, lnx_w, lnx_b):
    B, S, _ = u.shape
    H, N, C = RWKV_HEADS, HEAD_DIM, RWKV_WIDTH
    u = u.astype(jnp.float32)
    prev = jnp.pad(u, ((0, 0), (1, 0), (0, 0)))[:, :-1]
    nxt = jnp.pad(u, ((0, 0), (0, 1), (0, 0)))[:, 1:]
    u = u + mu_prev * (prev - u) + mu_next * (nxt - u)
    cuts = np.cumsum([C, C, C, N_DIRS * DECAY_LORA, N_DIRS * ICLR_LORA]).tolist()
    r, k, v, wd, ad, gd = jnp.split(u, cuts, axis=-1)
    wd = wd.reshape(B, S, N_DIRS, DECAY_LORA)
    ad = ad.reshape(B, S, N_DIRS, ICLR_LORA)
    w_logit = w0 + jnp.einsum('bsdr,drc->bsdc', jnp.tanh(wd), w2)
    decay = jnp.exp(-jnp.exp(-jax.nn.softplus(-w_logit) - 0.5))
    a = jax.nn.sigmoid(a0 + jnp.einsum('bsdr,drc->bsdc', ad, a2))
    g = jax.nn.sigmoid(gd) @ g2
    kk = (k * k_k).reshape(B, S, H, N)
    kk = kk / jnp.maximum(jnp.sqrt(jnp.sum(kk * kk, axis=-1, keepdims=True)), 1e-12)
    kk = kk.reshape(B, S, C)
    k_dir = k[:, :, None, :] * (1.0 + (a - 1.0) * k_a)

    def both(t):
        return jnp.broadcast_to(t[:, :, None, :], (B, S, N_DIRS, C))

    def orient(t):
        t = jnp.concatenate([t[:, :, :1], jnp.flip(t[:, :, 1:], axis=1)], axis=2)
        return t.reshape(B, S, N_DIRS, H, N).transpose(1, 2, 0, 3, 4)

    xs = (orient(both(r)), orient(decay), orient(k_dir), orient(both(v)),
          orient(both(kk)), orient(kk[:, :, None, :] * a))
    state0 = jnp.zeros((N_DIRS, B, H, N, N), jnp.float32)
    _, ys = lax.scan(_rwkv7_step, state0, xs)
    ys = ys.transpose(2, 0, 1, 3, 4)
    y = ys[:, :, 0] + jnp.flip(ys[:, :, 1], axis=1)
    mu = jnp.mean(y, axis=-1, keepdims=True)
    var = jnp.mean(jnp.square(y - mu), axis=-1, keepdims=True)
    y = ((y - mu) * lax.rsqrt(var + GN_EPS)).reshape(B, S, C) * lnx_w + lnx_b
    bonus = jnp.einsum('bshn,bsdhn,hn->bsh', r.reshape(B, S, H, N),
                       k_dir.reshape(B, S, N_DIRS, H, N), r_k) / N_DIRS
    y = y + (bonus[..., None] * v.reshape(B, S, H, N)).reshape(B, S, C)
    return y * g

def first_inputs(seed: int = 0) -> dict:
    key = jax.random.key(seed)
    keys = iter(jax.random.split(key, 40))

    def rnd(shape, scale):
        return scale * jax.random.normal(next(keys), (DEPTH,) + shape, jnp.float32)

    def gain(shape):
        return 1.0 + rnd(shape, 0.05)

    def unif(shape, lo, hi):
        return jax.random.uniform(next(keys), (DEPTH,) + shape, jnp.float32, lo, hi)

    x = jax.random.normal(next(keys), (BATCH, SEQ, D_MODEL), jnp.float32)
    return {
        "x": x,
        "ffn1_pre_g": gain((D_MODEL,)),
        "ffn1_w_gate": rnd((D_MODEL, D_FF), D_MODEL ** -0.5),
        "ffn1_w_up": rnd((D_MODEL, D_FF), D_MODEL ** -0.5),
        "ffn1_w_down": rnd((D_FF, D_MODEL), D_FF ** -0.5),
        "ffn1_post_g": gain((D_MODEL,)),
        "mix_pre_g": gain((D_MODEL,)),
        "w_in": rnd((D_MODEL, IN_WIDTH), D_MODEL ** -0.5),
        "rwkv_mu_prev": unif((RWKV_IN,), 0.0, 0.5),
        "rwkv_mu_next": unif((RWKV_IN,), 0.0, 0.5),
        "rwkv_w0": unif((N_DIRS, RWKV_WIDTH), -4.0, 1.0),
        "rwkv_w2": rnd((N_DIRS, DECAY_LORA, RWKV_WIDTH), 0.5 * DECAY_LORA ** -0.5),
        "rwkv_a0": rnd((N_DIRS, RWKV_WIDTH), 0.3),
        "rwkv_a2": rnd((N_DIRS, ICLR_LORA, RWKV_WIDTH), 0.5 * ICLR_LORA ** -0.5),
        "rwkv_g2": rnd((GATE_LORA, RWKV_WIDTH), GATE_LORA ** -0.5),
        "rwkv_k_k": 0.85 + rnd((RWKV_WIDTH,), 0.05),
        "rwkv_k_a": gain((RWKV_WIDTH,)),
        "rwkv_r_k": rnd((RWKV_HEADS, HEAD_DIM), 0.1),
        "rwkv_lnx_w": gain((RWKV_WIDTH,)),
        "rwkv_lnx_b": rnd((RWKV_WIDTH,), 0.02),
        "attn_out_g": gain((ATT_WIDTH,)),
        "w_out": rnd((MIX_WIDTH, D_MODEL), MIX_WIDTH ** -0.5),
        "mix_post_g": gain((D_MODEL,)),
        "ffn2_pre_g": gain((D_MODEL,)),
        "ffn2_w_gate": rnd((D_MODEL, D_FF), D_MODEL ** -0.5),
        "ffn2_w_up": rnd((D_MODEL, D_FF), D_MODEL ** -0.5),
        "ffn2_w_down": rnd((D_FF, D_MODEL), D_FF ** -0.5),
        "ffn2_post_g": gain((D_MODEL,)),
    }

def first_block(x, ffn1_pre_g, ffn1_w_gate, ffn1_w_up, ffn1_w_down, ffn1_post_g,
              mix_pre_g, w_in,
              rwkv_mu_prev, rwkv_mu_next, rwkv_w0, rwkv_w2, rwkv_a0, rwkv_a2, rwkv_g2,
              rwkv_k_k, rwkv_k_a, rwkv_r_k, rwkv_lnx_w, rwkv_lnx_b,
              attn_out_g, w_out, mix_post_g,
              ffn2_pre_g, ffn2_w_gate, ffn2_w_up, ffn2_w_down, ffn2_post_g):
    S = x.shape[1]
    pos = jnp.arange(S, dtype=jnp.float32)
    inv_freq = ROPE_THETA ** (-jnp.arange(0, HEAD_DIM, 2, dtype=jnp.float32) / HEAD_DIM)
    ang = pos[:, None] * inv_freq[None, :]
    cos, sin = jnp.cos(ang), jnp.sin(ang)

    h = x.astype(jnp.float32)
    for l in range(DEPTH):
        f = _swiglu(_rmsnorm(h, ffn1_pre_g[l]), ffn1_w_gate[l], ffn1_w_up[l], ffn1_w_down[l])
        h = h + 0.5 * _rmsnorm(f, ffn1_post_g[l])
        z = _rmsnorm(h, mix_pre_g[l]) @ w_in[l]
        y_att = _attention_group(z[..., :ATT_IN], cos, sin, attn_out_g[l])
        y_rwkv = _rwkv7_group(z[..., ATT_IN:], rwkv_mu_prev[l], rwkv_mu_next[l], rwkv_w0[l], rwkv_w2[l],
                              rwkv_a0[l], rwkv_a2[l], rwkv_g2[l], rwkv_k_k[l], rwkv_k_a[l], rwkv_r_k[l],
                              rwkv_lnx_w[l], rwkv_lnx_b[l])
        mix = jnp.concatenate([y_att, y_rwkv], axis=-1) @ w_out[l]
        h = h + _rmsnorm(mix, mix_post_g[l])
        f = _swiglu(_rmsnorm(h, ffn2_pre_g[l]), ffn2_w_gate[l], ffn2_w_up[l], ffn2_w_down[l])
        h = h + 0.5 * _rmsnorm(f, ffn2_post_g[l])
    return h.astype(x.dtype)


DEPTH_2 = 2

GRID_W = 64
CTX_LEN = 256
ATT_KV_HEADS = 2
ATT_HEAD_DIM = 64
ATT_GROUP = ATT_HEADS // ATT_KV_HEADS
WINDOW = 128
ATT_BLOCK = 128
ATT_SPAN = ATT_BLOCK + 2 * WINDOW
ML_HEADS = 4
ML_QK_DIM = 64
ML_V_DIM = 128
ML_CHUNK = 64
ML_CONV = 5
GATE_CAP = 15.0
ATT_WIDTH_2 = ATT_HEADS * ATT_HEAD_DIM
ATT_KV_WIDTH = ATT_KV_HEADS * ATT_HEAD_DIM
ML_QK_WIDTH = ML_HEADS * ML_QK_DIM
ML_WIDTH = ML_HEADS * ML_V_DIM
ML_GATES = 4 * ML_HEADS
MIX_WIDTH_2 = ATT_WIDTH_2 + ML_WIDTH
SPLIT_SIZES = (ATT_WIDTH_2, ATT_KV_WIDTH, ATT_KV_WIDTH, ML_QK_WIDTH, ML_QK_WIDTH, ML_WIDTH, ML_WIDTH, ML_GATES)
IN_WIDTH_2 = ATT_WIDTH_2 + 2 * ATT_KV_WIDTH + 2 * ML_QK_WIDTH + 2 * ML_WIDTH + ML_GATES
FFN_DIM = 2816
N_EXPERTS = 8
TOP_K = 2
EPS = 1e-6


def rmsnorm(x, g):
    xf = x.astype(jnp.float32)
    y = xf * lax.rsqrt(jnp.mean(xf * xf, axis=-1, keepdims=True) + EPS)
    return (y * g.astype(jnp.float32)).astype(x.dtype)

def adaln(x, g, shift, scale):
    return rmsnorm(x, g) * (1 + scale) + shift

def split_columns(u):
    points = [int(p) for p in np.cumsum(SPLIT_SIZES)[:-1]]
    return jnp.split(u, points, axis=-1)

def axial_rope_tables(n_tokens):
    rows = n_tokens // GRID_W
    t = jnp.arange(rows * GRID_W)
    row = jnp.repeat(jnp.arange(rows), GRID_W).astype(jnp.float32)
    col = (t % GRID_W).astype(jnp.float32)
    quarter = ATT_HEAD_DIM // 4
    inv = ROPE_THETA ** (-jnp.arange(quarter, dtype=jnp.float32) / quarter)
    ang_r = row[:, None] * inv[None, :]
    ang_c = col[:, None] * inv[None, :]
    return (jnp.cos(ang_r), jnp.sin(ang_r), jnp.cos(ang_c), jnp.sin(ang_c))

def _rotate_half(x, cos, sin):
    x1, x2 = jnp.split(x, 2, axis=-1)
    return jnp.concatenate([x1 * cos - x2 * sin, x2 * cos + x1 * sin], axis=-1)

def apply_axial_rope(x, tabs):
    cos_r, sin_r, cos_c, sin_c = [t[:, None, :] for t in tabs]
    xf = x.astype(jnp.float32)
    half = x.shape[-1] // 2
    out = jnp.concatenate([_rotate_half(xf[..., :half], cos_r, sin_r),
                           _rotate_half(xf[..., half:], cos_c, sin_c)], axis=-1)
    return out.astype(x.dtype)

def sink_attention(qg, kv_sets, sink_g):
    sink = sink_g[None, :, :, None]
    m = sink
    scores = []
    for k, v, mask in kv_sets:
        s = jnp.einsum('bqhgd,bkhd->bhgqk', qg, k).astype(jnp.float32)
        if mask is not None:
            s = jnp.where(mask, s, -jnp.inf)
        scores.append(s)
        m = jnp.maximum(m, s.max(-1))
    denom = jnp.exp(sink - m)
    num = None
    for s, (k, v, mask) in zip(scores, kv_sets):
        p = jnp.exp(s - m[..., None])
        denom = denom + p.sum(-1)
        o = jnp.einsum('bhgqk,bkhd->bhgqd', p, v.astype(jnp.float32))
        num = o if num is None else num + o
    out = num / denom[..., None]
    return jnp.transpose(out, (0, 3, 1, 2, 4))

def window_attention(q, k, v, k_ctx, v_ctx, sink_g):
    B, S = q.shape[:2]
    nb = S // ATT_BLOCK
    qg = (q * (ATT_HEAD_DIM ** -0.5)).reshape(B, nb, ATT_BLOCK, ATT_KV_HEADS, ATT_GROUP, ATT_HEAD_DIM)
    pad = ((0, 0), (WINDOW, WINDOW), (0, 0), (0, 0))
    kp = jnp.pad(k, pad)
    vp = jnp.pad(v, pad)
    valid = jnp.pad(jnp.ones((S,), dtype=bool), (WINDOW, WINDOW))
    rel = jnp.abs(jnp.arange(ATT_BLOCK)[:, None] + WINDOW - jnp.arange(ATT_SPAN)[None, :]) <= WINDOW

    def block(j):
        start = j * ATT_BLOCK
        qb = lax.dynamic_index_in_dim(qg, j, axis=1, keepdims=False)
        kb = lax.dynamic_slice_in_dim(kp, start, ATT_SPAN, axis=1)
        vb = lax.dynamic_slice_in_dim(vp, start, ATT_SPAN, axis=1)
        mask = rel & lax.dynamic_slice_in_dim(valid, start, ATT_SPAN)[None, :]
        out = sink_attention(qb, ((kb, vb, mask), (k_ctx, v_ctx, None)), sink_g)
        return out.reshape(B, ATT_BLOCK, ATT_WIDTH_2).astype(q.dtype)

    outs = lax.map(block, jnp.arange(nb))
    return jnp.moveaxis(outs, 0, 1).reshape(B, S, ATT_WIDTH_2)

def mlstm_chunkwise(q, k, v, i_pre, f_pre, state):
    B, T, H, DK = q.shape
    DV = v.shape[-1]
    nc = T // ML_CHUNK
    f32 = jnp.float32

    def chunks(a):
        return jnp.moveaxis(a.reshape((B, nc, ML_CHUNK) + a.shape[2:]), 1, 0)

    qs = chunks(q.astype(f32) * (DK ** -0.5))
    ks = chunks(k.astype(f32))
    vs = chunks(v.astype(f32))
    lis = chunks(i_pre.astype(f32))
    lfs = chunks(jax.nn.log_sigmoid(f_pre.astype(f32)))
    causal = jnp.tril(jnp.ones((ML_CHUNK, ML_CHUNK), dtype=bool))

    def step(carry, inp):
        C, n, m = carry
        qc, kc, vc, li, lf = inp
        b = jnp.cumsum(lf, axis=1).transpose(0, 2, 1)
        ig = li.transpose(0, 2, 1)
        d = jnp.where(causal, b[..., :, None] - b[..., None, :] + ig[..., None, :], -jnp.inf)
        inter = b + m[..., None]
        m_t = jnp.maximum(inter, d.max(-1))
        w_inter = jnp.exp(inter - m_t)
        s = jnp.einsum('bthd,bshd->bhts', qc, kc) * jnp.exp(d - m_t[..., None])
        num = jnp.einsum('bhts,bshe->bhte', s, vc) + w_inter[..., None] * jnp.einsum('bthd,bhde->bhte', qc, C)
        den = s.sum(-1) + w_inter * jnp.einsum('bthd,bhd->bht', qc, n)
        h = num / jnp.maximum(jnp.abs(den), jnp.exp(-m_t))[..., None]
        b_end = b[..., -1]
        g = b_end[..., None] - b + ig
        m_new = jnp.maximum(b_end + m, g.max(-1))
        decay = jnp.exp(b_end + m - m_new)
        wk = jnp.exp(g - m_new[..., None])
        C_new = decay[..., None, None] * C + jnp.einsum('bhs,bshd,bshe->bhde', wk, kc, vc)
        n_new = decay[..., None] * n + jnp.einsum('bhs,bshd->bhd', wk, kc)
        return (C_new, n_new, m_new), h.transpose(0, 2, 1, 3)

    state, hs = lax.scan(step, state, (qs, ks, vs, lis, lfs))
    h = jnp.moveaxis(hs, 0, 1).reshape(B, T, H, DV)
    return h, state

def depthwise_conv(x, w, b):
    C = x.shape[-1]
    y = lax.conv_general_dilated(x, w.reshape(ML_CONV, 1, C).astype(x.dtype), (1,),
                                 [(ML_CONV // 2, ML_CONV // 2)],
                                 dimension_numbers=('NWC', 'WIO', 'NWC'), feature_group_count=C)
    return y + b

def mlstm_inputs(qm, km, vm, gt, conv_w, conv_b, b_gates):
    B, T, _ = qm.shape
    qk = jax.nn.silu(depthwise_conv(jnp.concatenate([qm, km], axis=-1), conv_w, conv_b))
    q, k = jnp.split(qk, 2, axis=-1)
    q = q.reshape(B, T, ML_HEADS, ML_QK_DIM)
    k = k.reshape(B, T, ML_HEADS, ML_QK_DIM)
    v = vm.reshape(B, T, ML_HEADS, ML_V_DIM)
    g = gt.astype(jnp.float32) + b_gates.astype(jnp.float32)
    g = (GATE_CAP * jnp.tanh(g / GATE_CAP)).reshape(B, T, 4, ML_HEADS)
    return q, k, v, g[:, :, 0], g[:, :, 1], g[:, :, 2], g[:, :, 3]

def init_state(B):
    f32 = jnp.float32
    return (jnp.zeros((B, ML_HEADS, ML_QK_DIM, ML_V_DIM), f32),
            jnp.zeros((B, ML_HEADS, ML_QK_DIM), f32),
            jnp.zeros((B, ML_HEADS), f32))

def merge_groups(att, h_ml, o_pre, g_att, g_ml, w_out):
    B, T = att.shape[:2]
    att_n = rmsnorm(att, g_att)
    hf = h_ml.astype(jnp.float32)
    hn = hf * lax.rsqrt(jnp.mean(hf * hf, axis=-1, keepdims=True) + EPS)
    hn = hn * g_ml.astype(jnp.float32).reshape(ML_HEADS, ML_V_DIM)
    ml = hn.reshape(B, T, ML_WIDTH).astype(att.dtype) * jax.nn.sigmoid(o_pre)
    return jnp.concatenate([att_n, ml], axis=-1) @ w_out

def token_mixing(hx, hc, w_in, conv_w, conv_b, b_gates, attn_sink, g_att, g_ml, w_out, rope, with_ctx_out):
    B, S, _ = hx.shape
    L = hc.shape[1]
    qa_x, ka_x, va_x, qm_x, km_x, vm_x, om_x, gt_x = split_columns(hx @ w_in)
    qa_c, ka_c, va_c, qm_c, km_c, vm_c, om_c, gt_c = split_columns(hc @ w_in)
    sink_g = attn_sink.astype(jnp.float32).reshape(ATT_KV_HEADS, ATT_GROUP)
    k_ctx = ka_c.reshape(B, L, ATT_KV_HEADS, ATT_HEAD_DIM)
    v_ctx = va_c.reshape(B, L, ATT_KV_HEADS, ATT_HEAD_DIM)
    q = apply_axial_rope(qa_x.reshape(B, S, ATT_HEADS, ATT_HEAD_DIM), rope)
    k = apply_axial_rope(ka_x.reshape(B, S, ATT_KV_HEADS, ATT_HEAD_DIM), rope)
    v = va_x.reshape(B, S, ATT_KV_HEADS, ATT_HEAD_DIM)
    att_x = window_attention(q, k, v, k_ctx, v_ctx, sink_g)
    qc_, kc_, vc_, icf, fcf, icb, fcb = mlstm_inputs(qm_c, km_c, vm_c, gt_c, conv_w, conv_b, b_gates)
    qx_, kx_, vx_, ixf, fxf, ixb, fxb = mlstm_inputs(qm_x, km_x, vm_x, gt_x, conv_w, conv_b, b_gates)
    flip = lambda a: jnp.flip(a, axis=1)
    h_cf, st_f = mlstm_chunkwise(qc_, kc_, vc_, icf, fcf, init_state(B))
    h_cb, st_b = mlstm_chunkwise(flip(qc_), flip(kc_), flip(vc_), flip(icb), flip(fcb), init_state(B))
    h_xf, _ = mlstm_chunkwise(qx_, kx_, vx_, ixf, fxf, st_f)
    h_xb, _ = mlstm_chunkwise(flip(qx_), flip(kx_), flip(vx_), flip(ixb), flip(fxb), st_b)
    out_x = merge_groups(att_x, h_xf + flip(h_xb), om_x, g_att, g_ml, w_out)
    if not with_ctx_out:
        return out_x, None
    qg_c = (qa_c * (ATT_HEAD_DIM ** -0.5)).reshape(B, L, ATT_KV_HEADS, ATT_GROUP, ATT_HEAD_DIM)
    att_c = sink_attention(qg_c, ((k_ctx, v_ctx, None),), sink_g).reshape(B, L, ATT_WIDTH_2).astype(hc.dtype)
    out_c = merge_groups(att_c, h_cf + flip(h_cb), om_c, g_att, g_ml, w_out)
    return out_x, out_c

def swiglu(t, w1, w3, w2):
    return (jax.nn.silu(t @ w1) * (t @ w3)) @ w2

def moe_swiglu(h, w_router, b_router, w1, w3, w2):
    shp = h.shape
    t = h.reshape(-1, shp[-1])
    logits = (t @ w_router).astype(jnp.float32) + b_router.astype(jnp.float32)
    top_v, top_i = lax.top_k(logits, TOP_K)
    top_w = jax.nn.softmax(top_v, axis=-1)
    combine = jnp.sum(jax.nn.one_hot(top_i, N_EXPERTS, dtype=jnp.float32) * top_w[..., None], axis=1)
    y = None
    for e in range(N_EXPERTS):
        ye = combine[:, e:e + 1] * swiglu(t, w1[e], w3[e], w2[e]).astype(jnp.float32)
        y = ye if y is None else y + ye
    return y.astype(h.dtype).reshape(shp)

def channel_mix(h, layer, ffn_w1, ffn_w3, ffn_w2, w_router, b_router, exp_w1, exp_w3, exp_w2):
    i = layer // 2
    if layer % 2 == 0:
        return swiglu(h, ffn_w1[i], ffn_w3[i], ffn_w2[i])
    return moe_swiglu(h, w_router[i], b_router[i], exp_w1[i], exp_w3[i], exp_w2[i])

def second_inputs(seed: int = 0) -> dict:
    key = jax.random.key(seed)
    ks = jax.random.split(key, 26)
    D = D_MODEL
    n_dense = (DEPTH_2 + 1) // 2
    n_moe = DEPTH_2 // 2

    def nrm(i, shape, scale):
        return jax.random.normal(ks[i], shape, jnp.float32) * scale

    i_bias = -2.0 + nrm(11, (DEPTH_2, 2, ML_HEADS), 0.1)
    f_bias = 4.0 + nrm(12, (DEPTH_2, 2, ML_HEADS), 0.5)
    b_gates = jnp.stack([i_bias[:, 0], f_bias[:, 0], i_bias[:, 1], f_bias[:, 1]], axis=1).reshape(DEPTH_2, ML_GATES)
    return {
        'x': nrm(0, (BATCH, SEQ, D), 1.0),
        'c': nrm(1, (BATCH, D), 1.0),
        'ctx': nrm(2, (BATCH, CTX_LEN, D), 1.0),
        'c_ctx': nrm(3, (D,), 1.0),
        'norm1_g': 1.0 + nrm(4, (DEPTH_2, D), 0.02),
        'norm2_g': 1.0 + nrm(5, (DEPTH_2, D), 0.02),
        'w_mod': nrm(6, (DEPTH_2, D, 6 * D), 0.5 * D ** -0.5),
        'b_mod': nrm(7, (DEPTH_2, 6 * D), 0.02),
        'w_in': nrm(8, (DEPTH_2, D, IN_WIDTH_2), D ** -0.5),
        'conv_w': nrm(9, (DEPTH_2, ML_CONV, 2 * ML_QK_WIDTH), ML_CONV ** -0.5),
        'conv_b': nrm(10, (DEPTH_2, 2 * ML_QK_WIDTH), 0.02),
        'b_gates': b_gates,
        'attn_sink': nrm(13, (DEPTH_2, ATT_HEADS), 0.5),
        'g_att': 1.0 + nrm(14, (DEPTH_2, ATT_WIDTH_2), 0.02),
        'g_ml': 1.0 + nrm(15, (DEPTH_2, ML_WIDTH), 0.02),
        'w_out': nrm(16, (DEPTH_2, MIX_WIDTH_2, D), MIX_WIDTH_2 ** -0.5),
        'ffn_w1': nrm(17, (n_dense, D, FFN_DIM), D ** -0.5),
        'ffn_w3': nrm(18, (n_dense, D, FFN_DIM), D ** -0.5),
        'ffn_w2': nrm(19, (n_dense, FFN_DIM, D), FFN_DIM ** -0.5),
        'w_router': nrm(20, (n_moe, D, N_EXPERTS), D ** -0.5),
        'b_router': nrm(21, (n_moe, N_EXPERTS), 0.01),
        'exp_w1': nrm(22, (n_moe, N_EXPERTS, D, FFN_DIM), D ** -0.5),
        'exp_w3': nrm(23, (n_moe, N_EXPERTS, D, FFN_DIM), D ** -0.5),
        'exp_w2': nrm(24, (n_moe, N_EXPERTS, FFN_DIM, D), FFN_DIM ** -0.5),
        'final_g': 1.0 + nrm(25, (D,), 0.02),
    }

def second_block(x, c, ctx, c_ctx, norm1_g, norm2_g, w_mod, b_mod, w_in, conv_w, conv_b, b_gates,
              attn_sink, g_att, g_ml, w_out, ffn_w1, ffn_w3, ffn_w2, w_router, b_router,
              exp_w1, exp_w3, exp_w2, final_g):
    rope = axial_rope_tables(x.shape[1])
    cond_x = jax.nn.silu(c)
    cond_c = jax.nn.silu(c_ctx)[None]
    for layer in range(DEPTH_2):
        last = layer == DEPTH_2 - 1
        mod_x = jnp.split((cond_x @ w_mod[layer] + b_mod[layer])[:, None, :], 6, axis=-1)
        mod_c = jnp.split((cond_c @ w_mod[layer] + b_mod[layer])[:, None, :], 6, axis=-1)
        hx = adaln(x, norm1_g[layer], mod_x[0], mod_x[1])
        hc = adaln(ctx, norm1_g[layer], mod_c[0], mod_c[1])
        mix_x, mix_c = token_mixing(hx, hc, w_in[layer], conv_w[layer], conv_b[layer], b_gates[layer],
                                    attn_sink[layer], g_att[layer], g_ml[layer], w_out[layer], rope,
                                    not last)
        x = x + mod_x[2] * mix_x
        hx = adaln(x, norm2_g[layer], mod_x[3], mod_x[4])
        x = x + mod_x[5] * channel_mix(hx, layer, ffn_w1, ffn_w3, ffn_w2, w_router, b_router,
                                       exp_w1, exp_w3, exp_w2)
        if not last:
            ctx = ctx + mod_c[2] * mix_c
            hc = adaln(ctx, norm2_g[layer], mod_c[3], mod_c[4])
            ctx = ctx + mod_c[5] * channel_mix(hc, layer, ffn_w1, ffn_w3, ffn_w2, w_router, b_router,
                                               exp_w1, exp_w3, exp_w2)
    return rmsnorm(x, final_g)


def setup_inputs(seed=0):
    out = dict(first_inputs(seed))
    for name, value in second_inputs(seed + 1).items():
        if name != "x":
            out[name + "_2"] = value
    return out


def reference(
    x, ffn1_pre_g, ffn1_w_gate, ffn1_w_up, ffn1_w_down, ffn1_post_g, mix_pre_g, w_in,
    rwkv_mu_prev, rwkv_mu_next, rwkv_w0, rwkv_w2, rwkv_a0, rwkv_a2, rwkv_g2, rwkv_k_k, rwkv_k_a,
    rwkv_r_k, rwkv_lnx_w, rwkv_lnx_b, attn_out_g, w_out, mix_post_g, ffn2_pre_g, ffn2_w_gate,
    ffn2_w_up, ffn2_w_down, ffn2_post_g, c_2, ctx_2, c_ctx_2, norm1_g_2, norm2_g_2, w_mod_2,
    b_mod_2, w_in_2, conv_w_2, conv_b_2, b_gates_2, attn_sink_2, g_att_2, g_ml_2, w_out_2,
    ffn_w1_2, ffn_w3_2, ffn_w2_2, w_router_2, b_router_2, exp_w1_2, exp_w3_2, exp_w2_2,
    final_g_2,
):
    x = first_block(
        x, ffn1_pre_g, ffn1_w_gate, ffn1_w_up, ffn1_w_down, ffn1_post_g, mix_pre_g, w_in,
        rwkv_mu_prev, rwkv_mu_next, rwkv_w0, rwkv_w2, rwkv_a0, rwkv_a2, rwkv_g2, rwkv_k_k,
        rwkv_k_a, rwkv_r_k, rwkv_lnx_w, rwkv_lnx_b, attn_out_g, w_out, mix_post_g, ffn2_pre_g,
        ffn2_w_gate, ffn2_w_up, ffn2_w_down, ffn2_post_g,
    )
    return second_block(
        x, c_2, ctx_2, c_ctx_2, norm1_g_2, norm2_g_2, w_mod_2, b_mod_2, w_in_2, conv_w_2,
        conv_b_2, b_gates_2, attn_sink_2, g_att_2, g_ml_2, w_out_2, ffn_w1_2, ffn_w3_2,
        ffn_w2_2, w_router_2, b_router_2, exp_w1_2, exp_w3_2, exp_w2_2, final_g_2,
    )


_drawn_inputs = setup_inputs


def setup_inputs(seed=0):
    import zlib

    import numpy as np

    out = dict(_drawn_inputs(seed))
    spreads = {}
    factors = {'rwkv_w2': 3.92,
     'rwkv_k_k': 5.092,
     'rwkv_lnx_w': 3.326,
     'rwkv_lnx_b': 7.148,
     'ffn2_post_g': 3.32,
     'norm1_g_2': 8.0,
     'norm2_g_2': 4.446,
     'conv_b_2': 41.903,
     'attn_sink_2': 8.0,
     'g_att_2': 8.0,
     'g_ml_2': 8.0,
     'b_router_2': 8.0,
     'final_g_2': 8.055}
    for name, (base, spread) in spreads.items():
        noise = np.random.default_rng([zlib.crc32(name.encode()), seed]).standard_normal(out[name].shape)
        drawn = base * np.exp(spread * noise) if base else spread * noise
        out[name] = jnp.asarray(drawn.astype(out[name].dtype))
    for name, factor in factors.items():
        out[name] = (out[name] * factor).astype(out[name].dtype)
    return out
```

```python
from contextlib import ExitStack

import numpy as np
import concourse.bass as bass
from concourse import mybir

F32 = mybir.dt.float32
F32R = mybir.dt.float32r
U32 = mybir.dt.uint32
ALU = mybir.AluOpType
ACT = mybir.ActivationFunctionType
AX = mybir.AxisListType

P = 128
D = 1024
KT = D // P
S = 256
TT = S // P
FF = 2816
FT = FF // P
HD = 64
NH = 8
EXPERTS = 8
EPS = 1e-6
GN_EPS = 64e-5
RING = 12
CW = 1024
SPLIT = 6
SLOTS = 3
AHEAD = SPLIT - 1
NEG = -1e30
CH = 64
NC = S // CH


class Parts:
    pass


class Tally:

    def __init__(self, sem, table):
        self.sem, self.table, self.count = sem, table, 0

    def did(self, *name):
        self.count += 1
        if name:
            assert self.table.get((self.sem.name, name), self.count) == self.count, name
            self.table[(self.sem.name, name)] = self.count
        return self.sem, 1

    def at(self, *name):
        if self.table.get("complete"):
            return self.table[(self.sem.name, name)]
        return 1


def linked(engine, tally):
    def link(instruction, *name):
        instruction.then_inc(*tally.did(*name))
        engine.wait_ge(tally.sem, tally.count)
    return link



def vector_columns():
    sizes = [
        ("ffn1_pre_g", KT), ("mix_pre_g", KT), ("mu_prev", 15), ("mu_next", 15), ("w0", 8), ("a0", 8),
        ("k_k", 4), ("k_a", 4), ("r_k", 4), ("lnx_w", 4), ("lnx_b", 4), ("attn_out_g", 4),
        ("ffn2_pre_g", KT), ("norm1_g", 2 * KT), ("norm2_g", 2 * KT), ("b_mod", 2 * 48),
        ("conv_w", 2 * 5 * 4), ("conv_b", 2 * 4), ("gate_bias", 2 * 2), ("g_att", 2 * 4),
        ("g_ml", 2 * 4), ("cond", 2 * KT),
    ]
    at, out = 0, {}
    for name, n in sizes:
        out[name] = (at, n)
        at += n
    return out, at


def constant_columns():
    sizes = [
        ("ident", 128), ("ones", 128), ("rope1_swap", 128), ("rope2_swap", 128), ("head_ones", 128),
        ("rope1_cos", S), ("rope1_sin", S), ("rope2_cos", S), ("rope2_sin", S),
        ("dilated", TT * S), ("window", TT * S), ("chunk_keep", S),
        ("rwkv_masks", 2 * 5 * CH), ("chunk_eye", CH), ("tri", 2 * 128), ("pick_gate", 8 * 128), ("pick_expert", 8 * 128),
        ("experts", EXPERTS), ("pair_mask", 128),
    ]
    at, out = 0, {}
    for name, n in sizes:
        out[name] = (at, n)
        at += n
    return out, at


ROWS = ("ffn1_post_g", "mix_post_g", "ffn2_post_g", "final_g")



def meet(k):
    k.meetings += 1
    n = 4 * k.meetings

    def join(engine):
        engine.drain().then_inc(k.stage_done, 1)
        engine.wait_ge(k.stage_done, n)

    k.block.tensor(join)
    k.block.vector(join)
    k.block.scalar(join)
    k.block.gpsimd(join)


def take(k, shape):
    n = int(np.prod(shape[1:]))
    assert k.top + n <= k.arena_size, (k.top, n, k.arena_size)
    ap = k.arena[:, k.top:k.top + n]
    k.top += n
    if len(shape) == 3:
        ap = ap.rearrange("p (a b) -> p a b", a=shape[1])
    if len(shape) == 4:
        ap = ap.rearrange("p (a b c) -> p a b c", a=shape[1], b=shape[2])
    if len(shape) == 5:
        ap = ap.rearrange("p (a b c d) -> p a b c d", a=shape[1], b=shape[2], c=shape[3])
    return ap


def chunk_wait(k, pe, n, loop=None):
    fills = n // RING + 1
    pe.wait_ge(k.landed[n % RING], 16 * fills if loop is None else (loop + fills) * 16)


def rmsnorm_cm(k, tag, source, cols, gain, shift=None):
    nc = k.nc
    ssq, rstd, junk, xn = take(k, (P, TT)), take(k, (P, TT)), take(k, (P, TT, D)), take(k, (P, TT, D))
    pe_, dve_, act_ = k.pe, k.dve, k.act

    @k.block.scalar
    def _(act):
        for t in range(TT):
            nc.scalar.activation(junk[:, t, :], source[:, t, :], ACT.Square,
                                 accum_out=ssq[:, t:t + 1]).then_inc(*act_.did(tag, "ssq", t))
        act.wait_ge(dve_.sem, dve_.at(tag, "inv"))
        nc.scalar.activation(ssq, rstd, ACT.Sqrt).then_inc(*act_.did(tag, "rstd"))

    @k.block.vector
    def _(dve):
        link = linked(dve, dve_)
        dve.wait_ge(act_.sem, act_.at(tag, "ssq", TT - 1))
        link(nc.vector.tensor_scalar(ssq, ssq, 1.0 / D, EPS, ALU.mult, ALU.add))
        link(nc.vector.reciprocal(rstd, ssq), tag, "inv")
        dve.wait_ge(act_.sem, act_.at(tag, "rstd"))
        for t in range(TT):
            nc.vector.tensor_scalar(xn[:, t, :], source[:, t, :], ssq[:, t:t + 1], None,
                                    ALU.mult).then_inc(*dve_.did(tag, "xn", t))
        for kt in range(KT):
            dve.wait_ge(pe_.sem, pe_.at(tag, "turned", kt // 2))
            turned, out = k.psum[kt // 2][:, (kt % 2) * S:(kt % 2 + 1) * S], k.xt[:, kt, cols:cols + S]
            if shift is None:
                ins = nc.vector.tensor_scalar(out, turned, gain[:, kt:kt + 1], None, ALU.mult)
            else:
                ins = nc.vector.tensor_scalar(out, turned, gain[:, kt:kt + 1], shift[:, kt:kt + 1], ALU.mult, ALU.add)
            ins.then_inc(*dve_.did(tag, "xt", kt))

    @k.block.tensor
    def _(pe):
        pe.wait_ge(dve_.sem, dve_.at(tag, "xn", TT - 1))
        for kt in range(KT):
            for t in range(TT):
                c = (kt % 2) * S + t * P
                last = nc.tensor.transpose(k.psum[kt // 2][:, c:c + P], xn[:, t, kt * P:(kt + 1) * P], k.ident)
            if kt % 2:
                last.then_inc(*pe_.did(tag, "turned", kt // 2))


def round_steps(tiles):
    steps = []
    for j in range(tiles):
        steps += [("gate", j), ("up", j)]
        if j:
            steps.append(("down", j - 1))
    return steps + [("down", tiles - 1)]


def take_rounded(k, name, shape):
    at = k.top
    take(k, shape)
    return k.nc.alloc_sbuf_tensor_at(name, shape, F32R, offset=k.arena_base + 4 * at)[tuple(slice(None) for _ in shape)]


def split_high(k, act, n, loop, high):
    chunk_wait(k, act, n, loop)
    k.nc.scalar.copy(high, k.ring[:, n % RING, :]).then_inc(k.high_ready, 1)


def split_low(k, dve, n, loop, high, low, ready):
    dve.wait_ge(k.high_ready, ready)
    k.nc.vector.tensor_tensor(low, k.ring[:, n % RING, :], high.bitcast(F32), ALU.subtract).then_inc(k.chunk_used, 1)


def split_stage(k, tag, source, high, low, count, empty):
    nc, first, split0, pe_, dve_, act_ = k.nc, k.next_chunk, k.split_chunks, k.pe, k.dve, k.act
    w_high, w_low = take_rounded(k, tag + " w_high", (P, SLOTS, CW)), take_rounded(k, tag + " w_low", (P, SLOTS, CW))
    pieces = [slice(2 * n, 2 * n + 2) for n in range(KT // 2)]

    def chunk_high(act, q):
        if q >= SLOTS:
            act.wait_ge(pe_.sem, pe_.at(tag, "z", q - SLOTS))
        split_high(k, act, first + q, None, w_high[:, q % SLOTS, :])

    def chunk_low(dve, q):
        split_low(k, dve, first + q, None, w_high[:, q % SLOTS, :], w_low[:, q % SLOTS, :], split0 + q + 1)

    @k.block.scalar
    def _(act):
        for n, kts in enumerate(pieces):
            nc.scalar.copy(high[:, kts, :], source[:, kts, :]).then_inc(*act_.did(tag, "x", n))
            if n == 0:
                chunk_high(act, 0)
        chunk_high(act, 1)
        for n in range(count):
            if n + 2 < count:
                chunk_high(act, n + 2)
            empty(0, n)

    @k.block.vector
    def _(dve):
        for n, kts in enumerate(pieces):
            dve.wait_ge(act_.sem, act_.at(tag, "x", n))
            nc.vector.tensor_tensor(low[:, kts, :], source[:, kts, :], high[:, kts, :].bitcast(F32),
                                    ALU.subtract).then_inc(*dve_.did(tag, "x", n))
            if n == 0:
                chunk_low(dve, 0)
        chunk_low(dve, 1)
        for n in range(count):
            if n + 2 < count:
                chunk_low(dve, n + 2)
            empty(1, n)

    k.next_chunk += count
    k.split_chunks += count
    return w_high, w_low


def ffn(k, tag, cols, bodies, tail, experts=False):
    nc = k.nc
    silu, hidden = take(k, (P, 4, S)), take(k, (P, 4, S))
    scaled = take(k, (P, 4, S)) if experts else None
    assert k.top <= k.split_at
    first, tiles0, split0, used0 = k.next_chunk, k.ffn_tiles, k.split_chunks, k.ffn_chunks
    acc, bank = k.psum[0:4], k.psum[4:8]
    dve_, act_ = k.dve, k.act
    rounds = [(("loop", 4), bodies if tail else bodies - 1)] + [(("last", tail or 4), 1)]
    total = 3 * (4 * bodies + tail)

    def tiles_done(j, loop):
        return loop * 4 + (tiles0 + j + 1)

    def high(act, q, loop):
        used = used0 + q - SPLIT + 2
        if loop is not None:
            act.wait_ge(k.split_used, loop * RING + used)
        elif q >= SPLIT:
            act.wait_ge(k.split_used, used)
        split_high(k, act, first + q, loop, k.w_high[:, q % SPLIT, :])

    def low(dve, q, loop):
        ready = split0 + q + 1
        split_low(k, dve, first + q, loop, k.w_high[:, q % SPLIT, :], k.w_low[:, q % SPLIT, :],
                  ready if loop is None else loop * RING + ready)

    def each_round(engine, one):
        loops = rounds[0][1]
        with engine.Fori(0, loops) as i:
            one(4, i, 0, False)
        one(rounds[1][0][1], loops, RING * loops, True)

    def ahead(split, engine, p, loop, at, last):
        if not last:
            split(engine, p + AHEAD, loop)
        elif at + p + AHEAD < total:
            split(engine, at + p + AHEAD, None)

    @k.block.scalar
    def _(act):
        nc.scalar.copy(k.x_high[:, :, 0:S], k.xt[:, :, cols:cols + S]).then_inc(*act_.did(tag, "x"))

    @k.block.vector
    def _(dve):
        for n, a in enumerate(acc):
            nc.vector.memset(a[:, :], 0.0).then_inc(*dve_.did(tag, "clear", n))
        dve.wait_ge(act_.sem, act_.at(tag, "x"))
        nc.vector.tensor_tensor(k.x_low[:, :, 0:S], k.xt[:, :, cols:cols + S], k.x_high[:, :, 0:S].bitcast(F32),
                                ALU.subtract).then_inc(*dve_.did(tag, "x"))
        for q in range(AHEAD):
            low(dve, q, None)

        def gated(j, loop, expert):
            dve.wait_ge(k.silu_ready, tiles_done(j, loop))
            factor = silu
            if experts:
                nc.vector.tensor_tensor(scaled[:, j, :], silu[:, j, :],
                                        k.expert_weight[:, bass.ds(expert, S)], ALU.mult).then_inc(k.scaled_ready, 1)
                dve.wait_ge(k.scaled_ready, loop * 4 + (j + 1))
                factor = scaled
            nc.vector.tensor_tensor(hidden[:, j, :], factor[:, j, :], bank[j][:, S:2 * S],
                                    ALU.mult).then_inc(k.product_ready, 1)
            dve.wait_ge(k.product_ready, tiles_done(j, loop))
            nc.vector.tensor_copy(k.h_high[:, j, :], hidden[:, j, :]).then_inc(k.rounded_ready, 1)
            dve.wait_ge(k.rounded_ready, tiles_done(j, loop))
            nc.vector.tensor_tensor(k.h_low[:, j, :], hidden[:, j, :], k.h_high[:, j, :].bitcast(F32),
                                    ALU.subtract).then_inc(k.hidden_ready, 1)

        def one(count, loop, at, last, couple=0):
            for p, (what, j) in enumerate(round_steps(count)):
                ahead(low, dve, p, loop, at, last)
                if what == "up":
                    gated(j, loop, couple * (2 * S) + (j // 2) * S)

        if experts:
            per = FT // 2
            with dve.Fori(0, EXPERTS // 2 - 1) as e:
                with dve.Fori(0, per) as i:
                    one(4, e * per + i, 0, False, e)
            e = EXPERTS // 2 - 1
            with dve.Fori(e * per, e * per + per - 1) as i:
                one(4, i, 0, False, e)
            one(4, bodies - 1, RING * (bodies - 1), True, e)
        else:
            each_round(dve, one)

    @k.block.scalar
    def _(act):
        for q in range(AHEAD):
            high(act, q, None)

        def one(count, loop, at, last):
            for p, (what, j) in enumerate(round_steps(count)):
                ahead(high, act, p, loop, at, last)
                if what == "up":
                    act.wait_ge(k.gate_up_ready, tiles_done(j, loop))
                    nc.scalar.activation(silu[:, j, :], bank[j][:, 0:S], ACT.Silu).then_inc(k.silu_ready, 1)
        each_round(act, one)

    @k.block.tensor
    def _(pe):
        pe.wait_ge(dve_.sem, dve_.at(tag, "clear", 3))
        pe.wait_ge(dve_.sem, dve_.at(tag, "x"))

        def one(count, loop, at, last):
            after_up = False
            for p, (what, j) in enumerate(round_steps(count)):
                pe.wait_ge(k.chunk_used, loop * RING + (first + p + 1))
                slot = p % SPLIT
                wh, wl = k.w_high[:, slot, :], k.w_low[:, slot, :]
                if what == "down":
                    pe.wait_ge(k.hidden_ready, tiles_done(j, loop))
                    products = [(acc[2 * t + half][:, :], h[:, j, t * P:(t + 1) * P], w[:, 512 * half:512 * half + 512],
                                 False, True) for t in range(TT) for half in range(2)
                                for h, w in ((k.h_high, wh), (k.h_high, wl), (k.h_low, wh))]
                else:
                    out = bank[j][:, 0:S] if what == "gate" else bank[j][:, S:2 * S]
                    products = [(out, w[:, kt * P:(kt + 1) * P], x[:, kt, 0:S], kt == 0 and n == 0,
                                 kt == KT - 1 and n == 2) for kt in range(KT)
                                for n, (w, x) in enumerate(((wh, k.x_high), (wh, k.x_low), (wl, k.x_high)))]
                for m, (out, left, right, start, stop) in enumerate(products):
                    mm = nc.tensor.matmul(out, left, right, start=start, stop=stop,
                                          skip_group_check=what == "down")
                    if m == 0 and after_up:
                        mm.then_inc(k.split_used, 1)
                after_up = what == "up"
                mm.then_inc(k.gate_up_ready if what == "up" else k.split_used, 1)
        each_round(pe, one)

    k.next_chunk += total
    k.ffn_tiles += 4 * bodies + tail
    k.split_chunks += total
    k.ffn_chunks += total


def broadcast_row(k, row, out):
    @k.block.gpsimd
    def _(pool):
        pool.dma_start(out, k.rows[row:row + 1, 0:out.shape[1]].partition_broadcast(P)).then_inc(k.row_landed, 16)
    k.rows_loaded += 1
    return 16 * k.rows_loaded


def post_norm(k, tag, gain_row, factor, target):
    nc = k.nc
    f, junk = take(k, (P, TT, D)), take(k, (P, TT, D))
    part, ssq, rstd, gain = take(k, (P, TT, 2)), take(k, (P, TT)), take(k, (P, TT)), take(k, (P, D))
    dve_, act_ = k.dve, k.act
    loaded = broadcast_row(k, ROWS.index(gain_row), gain)

    @k.block.scalar
    def _(act):
        for t in range(TT):
            for half in range(2):
                nc.scalar.activation(junk[:, t, half * 512:(half + 1) * 512], k.psum[2 * t + half][:, :], ACT.Square,
                                     accum_out=part[:, t, half:half + 1]).then_inc(*act_.did(tag, "ssq", t, half))
        act.wait_ge(dve_.sem, dve_.at(tag, "inv"))
        nc.scalar.activation(ssq, rstd, ACT.Sqrt).then_inc(*act_.did(tag, "rstd"))

    @k.block.vector
    def _(dve):
        link = linked(dve, dve_)
        for t in range(TT):
            for half in range(2):
                dve.wait_ge(act_.sem, act_.at(tag, "ssq", t, half))
                nc.vector.tensor_copy(f[:, t, half * 512:(half + 1) * 512],
                                      k.psum[2 * t + half][:, :]).then_inc(*dve_.did(tag, "f", t, half))
        link(nc.vector.tensor_reduce(ssq, part, AX.X, ALU.add))
        link(nc.vector.tensor_scalar(ssq, ssq, 1.0 / D, EPS, ALU.mult, ALU.add))
        link(nc.vector.reciprocal(rstd, ssq), tag, "inv")
        dve.wait_ge(act_.sem, act_.at(tag, "rstd"))
        link(nc.vector.tensor_scalar(rstd, ssq, factor, None, ALU.mult))
        dve.wait_ge(k.row_landed, loaded)
        for t in range(TT):
            link(nc.vector.scalar_tensor_tensor(f[:, t, :], f[:, t, :], rstd[:, t:t + 1], gain, ALU.mult, ALU.mult))
            link(nc.vector.tensor_tensor(target[:, t, :], target[:, t, :], f[:, t, :], ALU.add))


def project(k, tag, cols, widths, out, high_at):
    nc, first, pe_, dve_ = k.nc, k.next_chunk, k.pe, k.dve
    copier = (k.act, k.dve)
    source = k.xt[:, :, cols:cols + max(widths)]
    x_low = take_rounded(k, tag + " x_low", (P, KT, max(widths)))
    keep, k.top = k.top, high_at
    x_high = take_rounded(k, tag + " x_high", (P, KT, max(widths)))
    k.top = keep

    def empty(engine, n):
        if n % 2 == engine:
            (nc.scalar, nc.vector)[engine].wait_ge(pe_.sem, pe_.at(tag, "z", n))
            copy = (nc.scalar.copy, nc.vector.tensor_copy)[engine]
            copy(out[:, n, 0:widths[n]], k.psum[n % 8][:, 0:widths[n]]).then_inc(*copier[engine].did(tag, "z", n))
    w_high, w_low = split_stage(k, tag, source, x_high, x_low, len(widths), empty)

    @k.block.tensor
    def _(pe):
        for n, width in enumerate(widths):
            pe.wait_ge(k.chunk_used, first + n + 1)
            if n >= 8:
                pe.wait_ge(copier[n % 2].sem, copier[n % 2].at(tag, "z", n - 8))
            wh, wl = w_high[:, n % SLOTS, :], w_low[:, n % SLOTS, :]
            for kt in range(KT):
                if n == 0 and kt % 2 == 0:
                    pe.wait_ge(dve_.sem, dve_.at(tag, "x", kt // 2))
                for m, (w, x) in enumerate(((wh, x_high), (wh, x_low), (wl, x_high))):
                    mm = nc.tensor.matmul(k.psum[n % 8][:, 0:width], w[:, kt * P:(kt + 1) * P], x[:, kt, 0:width],
                                          start=(kt == 0 and m == 0), stop=(kt == KT - 1 and m == 2))
            mm.then_inc(*pe_.did(tag, "z", n))


def rope(k, tag, z, tiles, swap, cos, sin):
    nc, pe_, dve_ = k.nc, k.pe, k.dve
    turned = take(k, (P, tiles, S))

    @k.block.tensor
    def _(pe):
        for t in range(tiles):
            nc.tensor.matmul(k.psum[t % 8][:, 0:S], swap, z[:, t, 0:S], start=True,
                             stop=True).then_inc(*pe_.did(tag, "swap", t))

    @k.block.vector
    def _(dve):
        for t in range(tiles):
            dve.wait_ge(pe_.sem, pe_.at(tag, "swap", t))
            nc.vector.tensor_tensor(turned[:, t, :], k.psum[t % 8][:, 0:S], sin, ALU.mult).then_inc(*dve_.did())
        for t in range(tiles):
            nc.vector.tensor_tensor(z[:, t, 0:S], z[:, t, 0:S], cos, ALU.mult).then_inc(*dve_.did())
        dve.wait_ge(dve_.sem, dve_.count)
        for t in range(tiles):
            nc.vector.tensor_tensor(z[:, t, 0:S], z[:, t, 0:S], turned[:, t, :], ALU.add).then_inc(*dve_.did())
        dve.wait_ge(dve_.sem, dve_.count)


def to_tokens(k, tag, source, tiles, out, token_tiles=TT):
    nc, pe_, act_ = k.nc, k.pe, k.act
    assert tiles <= 4

    @k.block.tensor
    def _(pe):
        for t in range(token_tiles):
            for c in range(tiles):
                mm = nc.tensor.transpose(k.psum[t][:, c * P:(c + 1) * P], source[:, c, t * P:(t + 1) * P], k.ident)
            mm.then_inc(*pe_.did(tag, "turned", t))

    @k.block.scalar
    def _(act):
        for t in range(token_tiles):
            act.wait_ge(pe_.sem, pe_.at(tag, "turned", t))
            nc.scalar.copy(out[:, t, 0:tiles * P], k.psum[t][:, 0:tiles * P]).then_inc(*act_.did(tag, "copied", t))


def to_channels(k, tag, source, tiles, out, gain, shift=None, token_tiles=TT):
    nc, pe_, dve_ = k.nc, k.pe, k.dve
    w = token_tiles * P

    @k.block.tensor
    def _(pe):
        for c in range(tiles):
            for t in range(token_tiles):
                mm = nc.tensor.transpose(k.psum[c][:, t * P:(t + 1) * P], source[:, t, c * P:(c + 1) * P], k.ident)
            mm.then_inc(*pe_.did(tag, "turned", c))

    @k.block.vector
    def _(dve):
        for c in range(tiles):
            dve.wait_ge(pe_.sem, pe_.at(tag, "turned", c))
            if shift is None:
                ins = nc.vector.tensor_scalar(out[:, c, 0:w], k.psum[c][:, 0:w], gain[:, c:c + 1], None, ALU.mult)
            else:
                ins = nc.vector.tensor_scalar(out[:, c, 0:w], k.psum[c][:, 0:w], gain[:, c:c + 1],
                                              shift[:, c:c + 1], ALU.mult, ALU.add)
            ins.then_inc(*dve_.did(tag, "out", c))


def inverse_root(k, tag, sums, n, eps, out):
    nc, dve_, act_ = k.nc, k.dve, k.act

    @k.block.vector
    def _(dve):
        link = linked(dve, dve_)
        link(nc.vector.tensor_scalar(sums, sums, 1.0 / n, eps, ALU.mult, ALU.add))
        link(nc.vector.reciprocal(sums, sums), tag, "inverse")

    @k.block.scalar
    def _(act):
        act.wait_ge(dve_.sem, dve_.at(tag, "inverse"))
        nc.scalar.activation(out, sums, ACT.Sqrt).then_inc(*act_.did(tag, "root"))


def dilated_attention(k, z, v_tm, mix_cm):
    nc, pe_, dve_, act_ = k.nc, k.pe, k.dve, k.act
    score, prob = take(k, (P, 2, TT * S)), take(k, (P, 2, TT * S))
    prob_t = take(k, (P, 2, TT * S))
    top, den, inv = take(k, (P, 2, TT)), take(k, (P, TT, NH)), take(k, (P, TT, NH))
    o, sq = take(k, (P, TT, 512)), take(k, (P, TT, 512))

    def head(h):
        return slice(HD * (h % 2), HD * (h % 2) + HD), h // 2

    @k.block.tensor
    def _(pe):
        for i in range(NH + 2):
            if i < NH:
                rows, tile = head(i)
                if i >= 2:
                    pe.wait_ge(dve_.sem, dve_.at("att1", "score", i - 2))
                for t in range(TT):
                    mm = nc.tensor.matmul(k.psum[i % 2][:, t * S:(t + 1) * S], z[rows, tile, t * P:(t + 1) * P],
                                          z[rows, 4 + tile, 0:S], start=True, stop=True)
                mm.then_inc(*pe_.did("att1", "score", i))
            h = i - 1
            if 0 <= h < NH:
                pe.wait_ge(act_.sem, act_.at("att1", "exp", h, TT - 1))
                if h >= 2:
                    pe.wait_ge(act_.sem, act_.at("att1", "prob_t", h - 2))
                for b in range(4):
                    mm = nc.tensor.transpose(k.psum[2 + h % 2][:, b * P:(b + 1) * P],
                                             prob[:, h % 2, b * P:(b + 1) * P], k.ident)
                mm.then_inc(*pe_.did("att1", "turned", h))
            h = i - 2
            if h >= 0:
                pe.wait_ge(act_.sem, act_.at("att1", "prob_t", h))
                for t in range(TT):
                    for b in range(TT):
                        mm = nc.tensor.matmul(k.psum[4 + t][:, h * HD:(h + 1) * HD],
                                              prob_t[:, h % 2, (2 * t + b) * P:(2 * t + b + 1) * P],
                                              v_tm[:, b, h * HD:(h + 1) * HD], start=(b == 0), stop=(b == 1))
                mm.then_inc(*pe_.did("att1", "value", h))

    @k.block.vector
    def _(dve):
        link = linked(dve, dve_)
        for h in range(NH):
            dve.wait_ge(pe_.sem, pe_.at("att1", "score", h))
            if h >= 2:
                dve.wait_ge(act_.sem, act_.at("att1", "exp", h - 2, TT - 1))
            link(nc.vector.scalar_tensor_tensor(score[:, h % 2, :], k.psum[h % 2][:, :], HD ** -0.5, k.c["dilated"],
                                                ALU.mult, ALU.add), "att1", "score", h)
            link(nc.vector.tensor_reduce(top[:, h % 2, :], score[:, h % 2, :].rearrange("p (t s) -> p t s", t=TT),
                                         AX.X, ALU.max))
            link(nc.vector.tensor_scalar(top[:, h % 2, :], top[:, h % 2, :], -1.0, None, ALU.mult), "att1", "top", h)
        dve.wait_ge(act_.sem, act_.at("att1", "exp", NH - 1, TT - 1))
        dve.wait_ge(pe_.sem, pe_.at("att1", "value", NH - 1))
        link(nc.vector.reciprocal(inv, den))
        for t in range(TT):
            ot = o[:, t, :].rearrange("p (h d) -> p h d", h=NH)
            link(nc.vector.tensor_tensor(ot, k.psum[4 + t][:, :].rearrange("p (h d) -> p h d", h=NH),
                                         inv[:, t, :].unsqueeze(2).to_broadcast([P, NH, HD]), ALU.mult))
        link(nc.vector.tensor_tensor(sq, o, o, ALU.mult))
        link(nc.vector.tensor_reduce(inv, sq.rearrange("p t (h d) -> p t h d", h=NH), AX.X, ALU.add))

    @k.block.scalar
    def _(act):
        for i in range(NH + 1):
            if i < NH:
                act.wait_ge(dve_.sem, dve_.at("att1", "top", i))
                if i >= 2:
                    act.wait_ge(pe_.sem, pe_.at("att1", "turned", i - 2))
                for t in range(TT):
                    nc.scalar.activation(prob[:, i % 2, t * S:(t + 1) * S], score[:, i % 2, t * S:(t + 1) * S], ACT.Exp,
                                         bias=top[:, i % 2, t:t + 1],
                                         accum_out=den[:, t, i:i + 1]).then_inc(*act_.did("att1", "exp", i, t))
            h = i - 1
            if h >= 0:
                act.wait_ge(pe_.sem, pe_.at("att1", "turned", h))
                if h >= 2:
                    act.wait_ge(pe_.sem, pe_.at("att1", "value", h - 2))
                nc.scalar.copy(prob_t[:, h % 2, :], k.psum[2 + h % 2][:, :]).then_inc(*act_.did("att1", "prob_t", h))

    inverse_root(k, "att1", inv, HD, EPS, inv)

    @k.block.vector
    def _(dve):
        dve.wait_ge(act_.sem, act_.at("att1", "root"))
        for t in range(TT):
            ot = o[:, t, :].rearrange("p (h d) -> p h d", h=NH)
            nc.vector.tensor_tensor(ot, ot, inv[:, t, :].unsqueeze(2).to_broadcast([P, NH, HD]),
                                    ALU.mult).then_inc(*dve_.did("att1", "normed", t))
    meet(k)
    to_channels(k, "att1 out", o, 4, mix_cm[:, 0:4, :], k.v["attn_out_g"])


def rwkv_inputs(k, z, low):
    nc, pe_, dve_, act_ = k.nc, k.pe, k.dve, k.act
    u = take(k, (P, 15, S))
    s = Parts()
    s.a, s.b, s.k, s.r = (take(k, (P, 2, 4, S)) for _ in range(4))
    s.gate, s.bonus = take(k, (P, 4, S)), take(k, (P, 4, S))
    s.v_tm = take(k, (P, TT, 512))
    s.y = take(k, (P, TT, 512))
    s.end = take(k, (P, 2, 4, NC))
    keep = s.keep = k.top

    own = take(k, (P, 15))

    @k.block.vector
    def _(dve):
        link = linked(dve, dve_)
        link(nc.vector.tensor_tensor(own, k.v["mu_prev"], k.v["mu_next"], ALU.add))
        link(nc.vector.tensor_scalar(own, own, -1.0, 1.0, ALU.mult, ALU.add))
        for j in range(15):
            nc.vector.tensor_scalar(u[:, j, :], z[:, j, :], own[:, j:j + 1], None, ALU.mult).then_inc(*dve_.did())
        dve.wait_ge(dve_.sem, dve_.count)
        for j in range(15):
            nc.vector.scalar_tensor_tensor(u[:, j, 1:S], z[:, j, 0:S - 1], k.v["mu_prev"][:, j:j + 1], u[:, j, 1:S],
                                           ALU.mult, ALU.add).then_inc(*dve_.did())
        dve.wait_ge(dve_.sem, dve_.count)
        for j in range(15):
            nc.vector.scalar_tensor_tensor(u[:, j, 0:S - 1], z[:, j, 1:S], k.v["mu_next"][:, j:j + 1],
                                           u[:, j, 0:S - 1], ALU.mult, ALU.add).then_inc(*dve_.did())
    meet(k)

    k.top = keep
    mats = take(k, (P, 3, 512))
    low_rank, opened, one_less = take(k, (P, S)), take(k, (P, S)), take(k, (P, 4))
    k.top = low
    decay, rate = take(k, (P, 2, 4, S)), take(k, (P, 2, 4, S))
    kk, tmp = take(k, (P, 4, S)), take(k, (P, 4, S))
    total = take(k, (P, 2, 4, S))
    assert k.top <= low + (KT + 28) * S
    r_, k_, v_ = u[:, 0:4, :], u[:, 4:8, :], u[:, 8:12, :]

    @k.block.gpsimd
    def _(pool):
        pool.dma_start(mats.rearrange("p a b -> p (a b)"), k.mats[:, 0:3 * 512]).then_inc(k.mats_landed, 16)

    @k.block.scalar
    def _(act):
        nc.scalar.activation(low_rank, u[:, 12, :], ACT.Tanh).then_inc(*act_.did("rw", "tanh"))
        nc.scalar.activation(opened, u[:, 14, :], ACT.Sigmoid).then_inc(*act_.did("rw", "open"))
        for n, (out, bias) in enumerate(((decay, "w0"), (rate, "a0"))):
            for d in range(2):
                for c in range(4):
                    act.wait_ge(pe_.sem, pe_.at("rw", "logit", n, d))
                    nc.scalar.activation(out[:, d, c, :], k.psum[4 * n + 2 * d + c // 2][:, (c % 2) * S:(c % 2 + 1) * S],
                                         ACT.Sigmoid, bias=k.v[bias][:, 4 * d + c:4 * d + c + 1]
                                         ).then_inc(*act_.did("rw", "rate", n, d, c))
        act.wait_ge(dve_.sem, dve_.at("rw", "kk norm"))
        nc.scalar.activation(tmp, tmp, ACT.Sqrt).then_inc(*act_.did("rw", "root"))

    @k.block.tensor
    def _(pe):
        pe.wait_ge(k.mats_landed, 16)
        pe.wait_ge(act_.sem, act_.at("rw", "tanh"))
        for n, source in enumerate((low_rank, u[:, 13, :])):
            for d in range(2):
                rows = slice(64 * d, 64 * d + 64)
                for c in range(4):
                    mm = nc.tensor.matmul(k.psum[4 * n + 2 * d + c // 2][:, (c % 2) * S:(c % 2 + 1) * S],
                                          mats[rows, n, c * P:(c + 1) * P], source[rows, :], start=True, stop=True)
                mm.then_inc(*pe_.did("rw", "logit", n, d))
        pe.wait_ge(act_.sem, act_.at("rw", "rate", 0, 1, 3))
        for c in range(4):
            mm = nc.tensor.matmul(k.psum[c // 2][:, (c % 2) * S:(c % 2 + 1) * S], mats[:, 2, c * P:(c + 1) * P],
                                  opened, start=True, stop=True)
        mm.then_inc(*pe_.did("rw", "gate"))
        pe.wait_ge(dve_.sem, dve_.at("rw", "kk sq"))
        for c in range(4):
            mm = nc.tensor.matmul(k.psum[2 + c // 2][:, (c % 2) * S:(c % 2 + 1) * S], k.c["head_ones"],
                                  tmp[:, c, :], start=True, stop=True)
        mm.then_inc(*pe_.did("rw", "kk sums"))
        pe.wait_ge(dve_.sem, dve_.at("rw", "bonus"))
        for c in range(4):
            mm = nc.tensor.matmul(k.psum[4 + c // 2][:, (c % 2) * S:(c % 2 + 1) * S], k.c["head_ones"],
                                  s.bonus[:, c, :], start=True, stop=True)
        mm.then_inc(*pe_.did("rw", "bonus sums"))

    @k.block.vector
    def _(dve):
        link = linked(dve, dve_)
        for c in range(4):
            nc.vector.tensor_scalar(kk[:, c, :], k_[:, c, :], k.v["k_k"][:, c:c + 1], None,
                                    ALU.mult).then_inc(*dve_.did())
        dve.wait_ge(dve_.sem, dve_.count)
        link(nc.vector.tensor_tensor(tmp, kk, kk, ALU.mult), "rw", "kk sq")
        link(nc.vector.tensor_scalar(one_less, k.v["k_a"], -1.0, 1.0, ALU.mult, ALU.add))
        dve.wait_ge(pe_.sem, pe_.at("rw", "kk sums"))
        for b in range(2):
            link(nc.vector.tensor_copy(tmp[:, 2 * b:2 * b + 2, :], k.psum[2 + b][:, :].rearrange(
                "p (c t) -> p c t", c=2)), "rw", *(("kk norm",) if b else ("kk half",)))
        dve.wait_ge(act_.sem, act_.at("rw", "root"))
        link(nc.vector.tensor_scalar(tmp, tmp, 1e-12, None, ALU.max))
        link(nc.vector.reciprocal(tmp, tmp))
        link(nc.vector.tensor_tensor(kk, kk, tmp, ALU.mult))
        for d in range(2):
            for c in range(4):
                nc.vector.tensor_scalar(s.k[:, d, c, :], rate[:, d, c, :], k.v["k_a"][:, c:c + 1], one_less[:, c:c + 1],
                                        ALU.mult, ALU.add).then_inc(*dve_.did())
        dve.wait_ge(dve_.sem, dve_.count)
        for d in range(2):
            nc.vector.tensor_tensor(s.k[:, d], s.k[:, d], k_, ALU.mult).then_inc(*dve_.did())
            nc.vector.tensor_tensor(s.b[:, d], rate[:, d], kk, ALU.mult).then_inc(*dve_.did())
        dve.wait_ge(dve_.sem, dve_.count)
        link(nc.vector.tensor_tensor(tmp, s.k[:, 0], s.k[:, 1], ALU.add))
        for c in range(4):
            nc.vector.scalar_tensor_tensor(s.bonus[:, c, :], r_[:, c, :], k.v["r_k"][:, c:c + 1], tmp[:, c, :],
                                           ALU.mult, ALU.mult).then_inc(*dve_.did("rw", *(("bonus",) if c == 3 else ("bonus", c))))
        link(nc.vector.tensor_scalar(decay, decay, -float(np.exp(-0.5)), None, ALU.mult))
        for d in range(2):
            for c in range(4):
                nc.vector.tensor_tensor_scan(total[:, d, c, :], k.c["chunk_keep"], decay[:, d, c, :], 0.0,
                                             ALU.mult, ALU.add).then_inc(*dve_.did())
        dve.wait_ge(dve_.sem, dve_.count)
        for d in range(2):
            link(nc.vector.tensor_copy(s.end[:, d], total[:, d].rearrange("p c (n t) -> p c n t", n=NC)[:, :, :, CH - 1]))
        for c in range(4):
            back, own_ = (x[:, 1, c, :].rearrange("p (n t) -> p n t", n=NC) for x in (total, decay))
            link(nc.vector.tensor_tensor(back, s.end[:, 1, c].unsqueeze(2).to_broadcast([P, NC, CH]), back,
                                         ALU.subtract))
            link(nc.vector.tensor_tensor(back, back, own_, ALU.add))
        link(nc.vector.tensor_tensor(decay, total, decay, ALU.subtract), "rw", "sums")
        for b in range(2):
            dve.wait_ge(pe_.sem, pe_.at("rw", "gate"))
            link(nc.vector.tensor_copy(s.gate[:, 2 * b:2 * b + 2, :], k.psum[b][:, :].rearrange("p (c t) -> p c t", c=2)))
        dve.wait_ge(pe_.sem, pe_.at("rw", "bonus sums"))
        for b in range(2):
            link(nc.vector.scalar_tensor_tensor(
                s.bonus[:, 2 * b:2 * b + 2, :].rearrange("p c t -> p (c t)"), k.psum[4 + b][:, :], 0.5,
                v_[:, 2 * b:2 * b + 2, :].rearrange("p c t -> p (c t)"), ALU.mult, ALU.mult))
        dve.wait_ge(act_.sem, act_.at("rw", "grown"))
        for d in range(2):
            link(nc.vector.tensor_tensor(s.a[:, d], decay[:, d], kk, ALU.mult))
            link(nc.vector.tensor_tensor(s.b[:, d], rate[:, d], s.b[:, d], ALU.mult))
            link(nc.vector.tensor_tensor(s.k[:, d], rate[:, d], s.k[:, d], ALU.mult))
            link(nc.vector.tensor_tensor(s.r[:, d], total[:, d], r_, ALU.mult))

    @k.block.scalar
    def _(act):
        act.wait_ge(dve_.sem, dve_.at("rw", "sums"))
        nc.scalar.activation(rate, total, ACT.Exp, scale=-1.0).then_inc(*act_.did("rw", "inverse"))
        nc.scalar.activation(decay, decay, ACT.Exp).then_inc(*act_.did("rw", "before"))
        nc.scalar.activation(s.end, s.end, ACT.Exp).then_inc(*act_.did("rw", "end"))
        act.wait_ge(act_.sem, act_.at("rw", "inverse"))
        nc.scalar.activation(total, total, ACT.Exp).then_inc(*act_.did("rw", "grown"))
    meet(k)
    k.top = keep
    to_tokens(k, "rw v", v_, 4, s.v_tm)
    meet(k)
    return s, u


MOD_TILES = 6 * KT
GAP = (12, 16, 16, 16, 20, 16, 16, 16, 20, 20, 24)
assert sum(GAP) * NC == 2 * MOD_TILES * KT


def modulate(k, pe, count):
    for _ in range(count):
        tile, kt = k.mod_products // KT, k.mod_products % KT
        layer, j = tile // MOD_TILES, tile % MOD_TILES
        n = k.mod_first + tile
        if kt == 0:
            chunk_wait(k, pe, n)
        mm = k.nc.tensor.matmul(k.psum[4][0:2 * MOD_TILES, layer * P:(layer + 1) * P],
                                k.cond[:, kt, 2 * (MOD_TILES - 1 - j):2 * (2 * MOD_TILES - 1 - j)],
                                k.ring[:, n % RING, kt * P:(kt + 1) * P], start=(j == 0 and kt == 0),
                                stop=(j == MOD_TILES - 1 and kt == KT - 1), skip_group_check=True)
        if kt == KT - 1:
            mm.then_inc(k.chunk_used, 1)
        k.mod_products += 1


def modulations(k):
    nc, pe_, dve_, act_ = k.nc, k.pe, k.dve, k.act
    rows = take(k, (P, 2 * P))

    @k.block.scalar
    def _(act):
        nc.scalar.copy(rows[0:2 * MOD_TILES, :], k.psum[4][0:2 * MOD_TILES, 0:2 * P]).then_inc(*act_.did("mod rows"))

    @k.block.tensor
    def _(pe):
        pe.wait_ge(act_.sem, act_.at("mod rows"))
        for layer in range(2):
            nc.tensor.transpose(k.psum[layer][:, 0:2 * MOD_TILES], rows[0:2 * MOD_TILES, layer * P:(layer + 1) * P],
                                k.ident[0:2 * MOD_TILES, 0:2 * MOD_TILES]).then_inc(*pe_.did("mod turned", layer))

    @k.block.vector
    def _(dve):
        link = linked(dve, dve_)
        for layer in range(2):
            dve.wait_ge(pe_.sem, pe_.at("mod turned", layer))
            for who in range(2):
                link(nc.vector.tensor_tensor(k.mod[:, layer, who, :],
                                             k.psum[layer][:, 0:96].rearrange("p (t w) -> p w t", w=2)[:, who, :],
                                             k.v["b_mod"][:, 48 * layer:48 * layer + 48], ALU.add))
            for norm, g in enumerate(("norm1_g", "norm2_g")):
                for who in range(2):
                    scale = k.mod[:, layer, who, 24 * norm + 8:24 * norm + 16]
                    gain = k.gain[:, layer, norm, who, :]
                    link(nc.vector.tensor_scalar(gain, scale, 1.0, None, ALU.add))
                    link(nc.vector.tensor_tensor(gain, gain, k.v[g][:, KT * layer:KT * layer + KT], ALU.mult))
    meet(k)


def rwkv_scan(k, s, u, low):
    nc, pe_, dve_, act_, pool_ = k.nc, k.pe, k.dve, k.act, k.pool
    k.top = s.keep
    wide_a, wide_r, wide_b = (take(k, (P, 2, 4, P)) for _ in range(3))
    state = take(k, (P, 2, 512))
    k.mod_first = k.next_chunk
    k.next_chunk += 2 * MOD_TILES
    k.top = low
    k_tm, b_tm = take(k, (P, 2, TT, 512)), take(k, (P, 2, TT, 512))
    end = take(k, (P, 2, 4, P))
    mask_n, mask_rb, mask_rk, q_off = (take(k, (P, 512)) for _ in range(4))
    k.cond = take(k, (P, KT, 4 * MOD_TILES - 2))
    assert k.top <= low + (KT + 28) * S
    u_flat = u.rearrange("p a b -> p (a b)")
    q0, q1, qt0, qt1, d0, d1, dt0 = (u_flat[:, 512 * j:512 * (j + 1)] for j in range(7))

    def heads(ap):
        return ap.rearrange("p (h t) -> p h t", h=8)

    def spread_heads(pool, i):
        link = linked(pool, pool_)
        for n, (wide, source) in enumerate(((wide_a, s.a), (wide_b, s.b), (wide_r, s.r))):
            for d, c in enumerate((i, NC - 1 - i)):
                for half in range(2):
                    r = slice(HD * half, HD * half + HD)
                    link(nc.gpsimd.tensor_copy(wide[r, d, :, HD * half:HD * half + HD],
                                               source[r, d, :, CH * c:CH * c + CH]), "wide", i, n, d, half)

    @k.block.tensor
    def _(pe):
        for n, source in enumerate((s.k, s.b)):
            for d in range(2):
                for t in range(TT):
                    bank = 4 * n + 2 * d + t
                    for c in range(4):
                        mm = nc.tensor.transpose(k.psum[bank][:, c * P:(c + 1) * P],
                                                 source[:, d, c, t * P:(t + 1) * P], k.ident)
                    mm.then_inc(*pe_.did("scan", "turned", bank))

    @k.block.scalar
    def _(act):
        for bank in range(0, 8, 2):
            act.wait_ge(pe_.sem, pe_.at("scan", "turned", bank))
            out = (k_tm, b_tm)[bank // 4][:, (bank // 2) % 2, bank % 2, :]
            nc.scalar.copy(out, k.psum[bank][:, :]).then_inc(*act_.did())

    @k.block.vector
    def _(dve):
        for bank in range(1, 8, 2):
            dve.wait_ge(pe_.sem, pe_.at("scan", "turned", bank))
            out = (k_tm, b_tm)[bank // 4][:, (bank // 2) % 2, bank % 2, :]
            nc.vector.tensor_copy(out, k.psum[bank][:, :]).then_inc(*dve_.did())
        nc.vector.memset(state, 0.0).then_inc(*dve_.did())

    @k.block.gpsimd
    def _(pool):
        for wide in (wide_a, wide_r, wide_b):
            nc.gpsimd.memset(wide, 0.0).then_inc(*pool_.did())
        nc.gpsimd.memset(k.cond, 0.0).then_inc(*pool_.did("cond"))
        pool.wait_ge(pool_.sem, pool_.at("cond"))
        spread_heads(pool, 0)

    @k.block.scalar
    def _(act):
        act.wait_ge(pool_.sem, pool_.at("cond"))
        nc.scalar.activation(k.cond[:, :, 2 * MOD_TILES - 2:2 * MOD_TILES],
                             k.v["cond"].rearrange("p (a b) -> p a b", a=KT), ACT.Silu).then_inc(*act_.did())
    meet(k)

    masks = k.c["rwkv_masks"].rearrange("p (a b c) -> p a b c", a=2, b=5)
    eye = k.c["chunk_eye"].unsqueeze(1).to_broadcast([P, 8, CH])

    for i in range(NC):
        chunk = (i, NC - 1 - i)
        base = [CH * (c % 2) for c in chunk]
        tile = [c // 2 for c in chunk]
        tokens = [slice(CH * c, CH * c + CH) for c in chunk]
        rows = [slice(b, b + CH) for b in base]
        bank = k.psum

        def each(pe, out, left, right, **how):
            for d in range(2):
                for h in range(8):
                    c = slice(CH * h, CH * h + CH)
                    mm = nc.tensor.matmul(out[rows[d], c], left[rows[d], c], right[rows[d], c],
                                          start=True, stop=True)
            return mm

        @k.block.gpsimd
        def _(pool):
            link = linked(pool, pool_)
            for d in range(2):
                link(nc.gpsimd.tensor_tensor(end[:, d], s.end[:, d, :, chunk[d]].unsqueeze(2).to_broadcast([P, 4, P]),
                                             k.c["pair_mask"].unsqueeze(1).to_broadcast([P, 4, P]), ALU.mult),
                     "end", i, d)
            if i + 1 < NC:
                pool.wait_ge(pe_.sem, pe_.at("products", i, 4))
                spread_heads(pool, i + 1)

        @k.block.tensor
        def _(pe):
            pe.wait_ge(pool_.sem, pool_.at("wide", i, 2, 1, 1))
            def product(n, out, left, right):
                for d in range(2):
                    for p in range(4):
                        mm = nc.tensor.matmul(bank[out][rows[d], p * P:(p + 1) * P], left[:, d, p, tokens[d]],
                                              right[:, d, p, :], start=True, stop=True)
                mm.then_inc(*pe_.did("products", i, n))
            product(0, 0, s.b, wide_a)
            product(1, 1, s.a, wide_b)
            product(2, 2, s.k, wide_a)
            product(3, 3, s.b, wide_r)
            modulate(k, pe, GAP[0])
            pe.wait_ge(dve_.sem, dve_.at("q", i))
            each(pe, bank[5], qt0, q0).then_inc(*pe_.did("square", i, 0))
            each(pe, bank[6], q0, qt0).then_inc(*pe_.did("square_t", i, 0))
            modulate(k, pe, GAP[1])
            for n in range(3):
                q, qt = ((q1, qt1), (q0, qt0))[n % 2]
                pe.wait_ge(dve_.sem, dve_.at("power", i, n))
                pe.wait_ge(act_.sem, act_.at("power_t", i, n))
                each(pe, bank[7], qt, d0).then_inc(*pe_.did("grow", i, n))
                each(pe, bank[0], q, dt0).then_inc(*pe_.did("grow_t", i, n))
                if n < 2:
                    each(pe, bank[5], qt, q).then_inc(*pe_.did("square", i, n + 1))
                    each(pe, bank[6], q, qt).then_inc(*pe_.did("square_t", i, n + 1))
                if n == 0:
                    pe.wait_ge(dve_.sem, dve_.at("mask", i, 3))
                    product(4, 3, s.k, wide_r)
                modulate(k, pe, GAP[2 + n])
            pe.wait_ge(dve_.sem, dve_.at("grown_t", i, 2))
            each(pe, bank[5], q_off, dt0).then_inc(*pe_.did("f", i))
            modulate(k, pe, GAP[5])
            pe.wait_ge(act_.sem, act_.at("f", i))
            for n in range(3):
                pe.wait_ge(dve_.sem, dve_.at("x", i, n - 1) if n else dve_.at("grown", i, 2))
                each(pe, bank[7], q0, d0 if n == 0 else d1).then_inc(*pe_.did("x", i, n))
                if n < 2:
                    modulate(k, pe, GAP[6 + n])
            for d in range(2):
                for p in range(4):
                    mm = nc.tensor.matmul(bank[5][rows[d], p * P:(p + 1) * P], s.a[:, d, p, tokens[d]],
                                          state[:, d, p * P:(p + 1) * P], start=True, stop=True)
                    for h in (2 * p, 2 * p + 1):
                        c = slice(CH * h, CH * h + CH)
                        mm = nc.tensor.matmul(bank[5][rows[d], c], mask_n[rows[d], c], s.v_tm[rows[d], tile[d], c],
                                              start=False, stop=True, skip_group_check=True)
            mm.then_inc(*pe_.did("rhs", i))
            modulate(k, pe, GAP[8])
            pe.wait_ge(dve_.sem, dve_.at("x", i, 2))
            pe.wait_ge(act_.sem, act_.at("rhs", i))
            each(pe, bank[6], d1, qt0).then_inc(*pe_.did("u", i))
            modulate(k, pe, GAP[9])
            pe.wait_ge(act_.sem, act_.at("u", i))
            for d in range(2):
                for p in range(4):
                    nc.tensor.matmul(bank[0][rows[d], p * P:(p + 1) * P], s.r[:, d, p, tokens[d]],
                                     state[:, d, p * P:(p + 1) * P], start=True, stop=True)
                    for h in (2 * p, 2 * p + 1):
                        c = slice(CH * h, CH * h + CH)
                        nc.tensor.matmul(bank[0][rows[d], c], mask_rk[rows[d], c], s.v_tm[rows[d], tile[d], c],
                                         start=False, stop=True, skip_group_check=True)
                        mm = nc.tensor.matmul(bank[0][rows[d], c], mask_rb[rows[d], c], qt1[rows[d], c],
                                              start=False, stop=True, skip_group_check=True)
            mm.then_inc(*pe_.did("y", i))
            for d in range(2):
                for p in range(4):
                    c = slice(p * P, (p + 1) * P)
                    nc.tensor.matmul(bank[1 + d][:, c], k_tm[rows[d], d, tile[d], c], s.v_tm[rows[d], tile[d], c],
                                     start=True, stop=False)
                    mm = nc.tensor.matmul(bank[1 + d][:, c], b_tm[rows[d], d, tile[d], c], qt1[rows[d], c],
                                          start=False, stop=True)
                mm.then_inc(*pe_.did("update", i, d))
            modulate(k, pe, GAP[10])

        @k.block.vector
        def _(dve):
            link = linked(dve, dve_)

            def masked(out, b, which):
                return nc.vector.tensor_tensor(heads(out), heads(bank[b][:, :]),
                                               masks[:, i % 2, which].unsqueeze(1).to_broadcast([P, 8, CH]), ALU.mult)
            dve.wait_ge(pe_.sem, pe_.at("products", i, 0))
            link(masked(q0, 0, 0))
            link(masked(q_off, 0, 1))
            dve.wait_ge(pe_.sem, pe_.at("products", i, 1))
            link(masked(qt0, 1, 2), "q", i)
            link(nc.vector.tensor_tensor(heads(d0), heads(q0), eye, ALU.add))
            link(nc.vector.tensor_tensor(heads(dt0), heads(qt0), eye, ALU.add))
            for n in range(3):
                q = (q1, q0)[n % 2]
                dve.wait_ge(pe_.sem, pe_.at("square", i, n))
                link(nc.vector.tensor_copy(q, bank[5][:, :]), "power", i, n)
                if n == 0:
                    for out, b, which in ((mask_n, 2, 3), (mask_rb, 3, 4)):
                        dve.wait_ge(pe_.sem, pe_.at("products", i, b))
                        link(masked(out, b, which), "mask", i, b)
                if n == 1:
                    dve.wait_ge(pe_.sem, pe_.at("products", i, 4))
                    link(masked(mask_rk, 3, 4), "mask", i, 4)
                dve.wait_ge(pe_.sem, pe_.at("grow", i, n))
                link(nc.vector.tensor_tensor(d0, d0, bank[7][:, :], ALU.add), "grown", i, n)
                dve.wait_ge(pe_.sem, pe_.at("grow_t", i, n))
                link(nc.vector.tensor_tensor(dt0, dt0, bank[0][:, :], ALU.add), "grown_t", i, n)
            for n in range(3):
                dve.wait_ge(pe_.sem, pe_.at("x", i, n))
                link(nc.vector.tensor_tensor(d1, d0, bank[7][:, :], ALU.add), "x", i, n)
            dve.wait_ge(pe_.sem, pe_.at("y", i))
            for d in range(2):
                out = s.y[rows[d], tile[d], :]
                if i < NC // 2:
                    link(nc.vector.tensor_copy(out, bank[0][rows[d], :]))
                else:
                    link(nc.vector.tensor_tensor(out, out, bank[0][rows[d], :], ALU.add))
            dve.wait_ge(pool_.sem, pool_.at("end", i, 1))
            for d in range(2):
                dve.wait_ge(pe_.sem, pe_.at("update", i, d))
                link(nc.vector.tensor_tensor(state[:, d, :], state[:, d, :], bank[1 + d][:, :], ALU.add))
                link(nc.vector.tensor_tensor(state[:, d, :], state[:, d, :], end[:, d].rearrange("p a b -> p (a b)"),
                                             ALU.mult), "state", i, d)

        @k.block.scalar
        def _(act):
            for n in range(3):
                qt = (qt1, qt0)[n % 2]
                act.wait_ge(pe_.sem, pe_.at("square_t", i, n))
                nc.scalar.copy(qt, bank[6][:, :]).then_inc(*act_.did("power_t", i, n))
            act.wait_ge(pe_.sem, pe_.at("f", i))
            nc.scalar.copy(q0, bank[5][:, :]).then_inc(*act_.did("f", i))
            act.wait_ge(pe_.sem, pe_.at("rhs", i))
            nc.scalar.copy(qt0, bank[5][:, :]).then_inc(*act_.did("rhs", i))
            act.wait_ge(pe_.sem, pe_.at("u", i))
            nc.scalar.mul(qt1, bank[6][:, :], -1.0).then_inc(*act_.did("u", i))
        meet(k)


def rwkv_output(k, s, low, mix_cm):
    nc, pe_, dve_, act_ = k.nc, k.pe, k.dve, k.act
    k.top = low
    sq, mean, var = take(k, (P, TT, 512)), take(k, (P, TT * NH)), take(k, (P, TT * NH))
    y = s.y.rearrange("p t (h d) -> p (t h) d", h=NH)

    def spread(ap):
        return ap.unsqueeze(2).to_broadcast([P, TT * NH, HD])

    @k.block.vector
    def _(dve):
        link = linked(dve, dve_)
        link(nc.vector.tensor_reduce(mean, y, AX.X, ALU.add))
        link(nc.vector.tensor_scalar(mean, mean, 1.0 / HD, None, ALU.mult))
        link(nc.vector.tensor_tensor(y, y, spread(mean), ALU.subtract))
        link(nc.vector.tensor_tensor(sq, s.y, s.y, ALU.mult))
        link(nc.vector.tensor_reduce(var, sq.rearrange("p t (h d) -> p (t h) d", h=NH), AX.X, ALU.add))
    inverse_root(k, "group norm", var, HD, GN_EPS, mean)

    @k.block.vector
    def _(dve):
        dve.wait_ge(act_.sem, act_.at("group norm", "root"))
        link = linked(dve, dve_)
        link(nc.vector.tensor_tensor(y, y, spread(mean), ALU.mult))
    meet(k)
    to_channels(k, "rwkv out", s.y, 4, mix_cm[:, 4:8, :], k.v["lnx_w"], k.v["lnx_b"])

    @k.block.vector
    def _(dve):
        dve.wait_ge(dve_.sem, dve_.count)
        link = linked(dve, dve_)
        link(nc.vector.tensor_tensor(mix_cm[:, 4:8, :], mix_cm[:, 4:8, :], s.bonus, ALU.add))
        link(nc.vector.tensor_tensor(mix_cm[:, 4:8, :], mix_cm[:, 4:8, :], s.gate, ALU.mult))
    meet(k)


def mix_down(k, tag, mix_cm, parts_at, token_tiles=TT):
    nc, first, pe_, dve_ = k.nc, k.next_chunk, k.pe, k.dve
    keep, k.top = k.top, parts_at
    m_high, m_low = (take_rounded(k, tag + name, (P, KT, token_tiles * P)) for name in (" m_high", " m_low"))
    k.top = keep
    w_high, w_low = split_stage(k, tag, mix_cm[:, :, 0:token_tiles * P], m_high, m_low, 8, lambda engine, n: None)

    @k.block.tensor
    def _(pe):
        for half in range(2):
            for part in range(4):
                n = 4 * half + part
                pe.wait_ge(k.chunk_used, first + n + 1)
                if half == 0:
                    pe.wait_ge(dve_.sem, dve_.at(tag, "x", part))
                wh, wl = (w[:, n % SLOTS, :].rearrange("p (k d) -> p k d", k=2) for w in (w_high, w_low))
                for t in range(token_tiles):
                    for kt in range(2):
                        for m, (x, w) in enumerate(((m_high, wh), (m_high, wl), (m_low, wh))):
                            mm = nc.tensor.matmul(k.psum[2 * t + half][:, :],
                                                  x[:, 2 * part + kt, t * P:(t + 1) * P], w[:, kt, :],
                                                  start=(part == 0 and kt == 0 and m == 0),
                                                  stop=(part == 3 and kt == 1 and m == 2))
                mm.then_inc(*pe_.did(tag, "z", n))



def build(nc, a, table, chunks, debug=None, stop=None):
    vcols, nv = vector_columns()
    ccols, ncst = constant_columns()
    with ExitStack() as ctx:
        enter = ctx.enter_context
        k = Parts()
        k.nc = nc
        k.stop = stop
        k.small_total = 48
        k.meetings = 0
        k.top = 0
        k.next_chunk = 0
        k.ffn_tiles = 0
        k.split_chunks = 0
        k.ffn_chunks = 0
        k.rows_loaded = 0
        k.mod_products = 0
        k.psum = [enter(nc.psum_tensor(f"bank{i}", [P, 512], F32)) for i in range(8)]
        k.ring = enter(nc.sbuf_tensor("weight_ring", [P, RING, CW], F32))
        k.const = enter(nc.sbuf_tensor("constants", [P, ncst], F32))
        k.vec = enter(nc.sbuf_tensor("vectors", [P, nv], F32))
        k.h = enter(nc.sbuf_tensor("x_residual", [P, TT, D], F32))[:, :, :]
        k.mod = enter(nc.sbuf_tensor("modulations", [P, 2, 2, 6 * KT], F32))
        k.gain = enter(nc.sbuf_tensor("norm_gains", [P, 2, 2, 2, KT], F32))
        k.arena_size, parts = 32144, {}
        k.arena_base = nc.sbuf_base if isinstance(nc.sbuf_base, int) else nc.sbuf_base()
        k.arena = enter(nc.sbuf_tensor("arena", [P, k.arena_size], F32))
        r_at = k.arena_size - 2 * SPLIT * CW - 2 * KT * S - 2 * 4 * S
        k.split_at = r_at
        for name, shape in (("w_high", (P, SPLIT, CW)), ("w_low", (P, SPLIT, CW)), ("x_high", (P, KT, S)),
                            ("x_low", (P, KT, S)), ("h_high", (P, 4, S)), ("h_low", (P, 4, S))):
            parts[name] = nc.alloc_sbuf_tensor_at(name, shape, F32R, offset=k.arena_base + 4 * r_at)
            r_at += shape[1] * shape[2]
        k.w_high, k.w_low, k.x_high, k.x_low, k.h_high, k.h_low = (
            parts[n][:, :, :] for n in ("w_high", "w_low", "x_high", "x_low", "h_high", "h_low"))
        k.rows, k.mats, k.ctx_in = a["rows"], a["matrices"], a["ctx"]
        k.landed = [enter(nc.semaphore(f"chunk_landed{i}")) for i in range(RING)]
        k.split_used = enter(nc.semaphore("split_used"))
        k.high_ready = enter(nc.semaphore("high_ready"))
        k.product_ready = enter(nc.semaphore("product_ready"))
        k.rounded_ready = enter(nc.semaphore("rounded_ready"))
        k.chunk_used = enter(nc.semaphore("chunk_used"))
        k.stage_done = enter(nc.semaphore("stage_done"))
        k.gate_up_ready = enter(nc.semaphore("gate_up_ready"))
        k.silu_ready = enter(nc.semaphore("silu_ready"))
        k.scaled_ready = enter(nc.semaphore("scaled_ready"))
        k.hidden_ready = enter(nc.semaphore("hidden_ready"))
        k.row_landed = enter(nc.semaphore("row_landed"))
        k.mats_landed = enter(nc.semaphore("mats_landed"))
        k.ctx_landed = enter(nc.semaphore("ctx_landed"))
        k.small_landed = enter(nc.semaphore("small_landed"))
        k.out_stored = enter(nc.semaphore("out_stored"))
        k.pe, k.dve, k.act, k.pool = (Tally(enter(nc.semaphore(f"{e}_steps")), table)
                                      for e in ("tensor", "vector", "scalar", "gpsimd"))
        k.c = {n: k.const[:, o:o + w] for n, (o, w) in ccols.items()}
        k.v = {n: k.vec[:, o:o + w] for n, (o, w) in vcols.items()}
        k.ident = k.c["ident"]
        k.block = enter(nc.Block())
        stream = a["stream"]

        @k.block.sync
        def _(sp):
            def fetch(n, slot):
                sp.dma_start(k.ring[:, slot, :], stream[n] if isinstance(n, int)
                             else stream[bass.ds(n, 1), :, :].rearrange("a p f -> p (a f)")).then_inc(k.landed[slot], 16)

            sp.dma_start(k.h[:, :, :], a["x"].rearrange("(t p) d -> p t d", p=P)).then_inc(k.small_landed, 16)
            sp.dma_start(k.vec[:, :], a["vectors"]).then_inc(k.small_landed, 16)
            sp.dma_start(k.const[:, :], a["constants"]).then_inc(k.small_landed, 16)
            for n in range(RING):
                fetch(n, n)
            whole = chunks // RING * RING
            if whole > RING:
                with sp.Fori(1, whole // RING) as r:
                    for slot in range(RING):
                        sp.wait_ge(k.chunk_used, r * RING + (slot + 1 - RING))
                        fetch(r * RING + slot, slot)
            for n in range(whole, chunks):
                sp.wait_ge(k.chunk_used, n + 1 - RING)
                fetch(n, n % RING)

        def loaded(engine):
            engine.wait_ge(k.small_landed, 48)
        for on in (k.block.tensor, k.block.vector, k.block.scalar, k.block.gpsimd):
            on(loaded)

        @k.block.tensor
        def _(pe):
            pe.sem_inc(k.split_used, 1)

        block_one(k)
        if k.stop is None:
            meet(k)
            block_two(k)
        if debug:
            debug(k, a)

        @k.block.scalar
        def _(act):
            act.dma_start(a["out"].rearrange("(t p) d -> p t d", p=P), k.h[:, :, :]).then_inc(k.out_stored, 16)
            act.wait_ge(k.out_stored, 16)
    table["chunks"] = k.next_chunk


def block_one(k):
    k.top = 0
    k.mix_cm = take(k, (P, KT, S))
    low = k.top
    k.xt = take(k, (P, KT, S))
    after_xt = k.top
    z = take(k, (P, 28, S))
    base = k.top
    rmsnorm_cm(k, "norm1", k.h, 0, k.v["ffn1_pre_g"])
    meet(k)
    k.top = after_xt
    ffn(k, "ffn1", 0, 5, 2)
    meet(k)
    k.top = base
    post_norm(k, "post1", "ffn1_post_g", 0.5, k.h)
    meet(k)
    k.top = base
    rmsnorm_cm(k, "norm2", k.h, 0, k.v["mix_pre_g"])
    meet(k)
    k.top = base
    k.top = base + KT * S
    project(k, "w_in", 0, [S] * 27, z, base)
    meet(k)
    rope(k, "rope", z, 8, k.c["rope1_swap"], k.c["rope1_cos"], k.c["rope1_sin"])
    meet(k)
    k.top = base
    v_tm = take(k, (P, TT, 512))
    to_tokens(k, "v", z[:, 8:12, :], 4, v_tm)
    meet(k)
    dilated_attention(k, z, v_tm, k.mix_cm)
    meet(k)
    k.top = base
    scan, u = rwkv_inputs(k, z[:, 12:27, :], low)
    rwkv_scan(k, scan, u, low)
    k.top = low
    modulations(k)
    rwkv_output(k, scan, low, k.mix_cm)
    if k.stop == "rwkv":
        return
    k.top = base
    mix_down(k, "w_out", k.mix_cm, after_xt)
    meet(k)
    k.top = base
    post_norm(k, "post2", "mix_post_g", 1.0, k.h)
    meet(k)
    k.top = base
    rmsnorm_cm(k, "norm3", k.h, 0, k.v["ffn2_pre_g"])
    meet(k)
    k.top = after_xt
    ffn(k, "ffn2", 0, 5, 2)
    meet(k)
    k.top = base
    post_norm(k, "post3", "ffn2_post_g", 0.5, k.h)
    meet(k)


def gate_rows(k, tag, who, which, out):
    nc, pe_, dve_ = k.nc, k.pe, k.dve
    diagonal = take(k, (P, KT, P))

    @k.block.vector
    def _(dve):
        for kt in range(KT):
            nc.vector.tensor_scalar(diagonal[:, kt, :], k.ident, k.mod[:, k.layer, who, which + kt:which + kt + 1], None,
                                    ALU.mult).then_inc(*dve_.did(tag, "diagonal", kt))
        for b in range(2):
            dve.wait_ge(pe_.sem, pe_.at(tag, "row", b))
            nc.vector.tensor_copy(out[:, 512 * b:512 * b + 512], k.psum[b][:, :]).then_inc(*dve_.did(tag, "row", b))

    @k.block.tensor
    def _(pe):
        pe.wait_ge(dve_.sem, dve_.at(tag, "diagonal", KT - 1))
        for b in range(2):
            nc.tensor.matmul(k.psum[b][:, :], k.c["ones"],
                             diagonal[:, 4 * b:4 * b + 4, :].rearrange("p a b -> p (a b)"), start=True,
                             stop=True).then_inc(*pe_.did(tag, "row", b))


def gated_add(k, tag, banks, gate, target):
    nc, dve_ = k.nc, k.dve
    tmp = take(k, (P, TT, D))

    @k.block.vector
    def _(dve):
        link = linked(dve, dve_)
        for t in range(TT):
            for half in range(2):
                c = slice(512 * half, 512 * half + 512)
                nc.vector.tensor_tensor(tmp[:, t, c], k.psum[banks + 2 * t + half][:, :], gate[:, c],
                                        ALU.mult).then_inc(*dve_.did())
        dve.wait_ge(dve_.sem, dve_.count)
        link(nc.vector.tensor_tensor(target, target, tmp, ALU.add))


def sink_attention(k, tag, z, cols, keys, v_tm, sink, mix_cm):
    nc, pe_, dve_, act_ = k.nc, k.pe, k.dve, k.act
    first_key = 0 if keys == 4 else TT
    width = keys * P
    keep = k.top
    score, prob, prob_t = take(k, (P, 2, width)), take(k, (P, 2, width)), take(k, (P, 2, width))
    top, den, inv = take(k, (P, TT, NH)), take(k, (P, TT, NH)), take(k, (P, TT, NH))
    sink_exp = take(k, (P, TT, NH))
    o, sq, ssq = take(k, (P, TT, 512)), take(k, (P, TT, 512)), take(k, (P, TT))
    units = [(h, t) for h in range(NH) for t in range(TT)]
    n = len(units)

    @k.block.tensor
    def _(pe):
        for i in range(n + 2):
            if i < n:
                h, t = units[i]
                rows = slice(HD * (h // 4), HD * (h // 4) + HD)
                if i >= 2:
                    pe.wait_ge(dve_.sem, dve_.at(tag, "score", i - 2))
                nc.tensor.matmul(k.psum[i % 2][:, 0:width], z[rows, h % 4, cols + t * P:cols + (t + 1) * P],
                                 z[rows, 4, first_key * P:first_key * P + width], start=True,
                                 stop=True).then_inc(*pe_.did(tag, "score", i))
            u = i - 1
            if 0 <= u < n:
                pe.wait_ge(act_.sem, act_.at(tag, "exp", u))
                if u >= 2:
                    pe.wait_ge(act_.sem, act_.at(tag, "prob_t", u - 2))
                for b in range(keys):
                    mm = nc.tensor.transpose(k.psum[2 + u % 2][:, b * P:(b + 1) * P],
                                             prob[:, u % 2, b * P:(b + 1) * P], k.ident)
                mm.then_inc(*pe_.did(tag, "turned", u))
            u = i - 2
            if u >= 0:
                h, t = units[u]
                pe.wait_ge(act_.sem, act_.at(tag, "prob_t", u))
                for b in range(keys):
                    mm = nc.tensor.matmul(k.psum[4 + t][:, h * HD:(h + 1) * HD], prob_t[:, u % 2, b * P:(b + 1) * P],
                                          v_tm[:, first_key + b, HD * (h // 4):HD * (h // 4) + HD],
                                          start=(b == 0), stop=(b == keys - 1))
                mm.then_inc(*pe_.did(tag, "value", u))

    @k.block.vector
    def _(dve):
        link = linked(dve, dve_)
        for i, (h, t) in enumerate(units):
            dve.wait_ge(pe_.sem, pe_.at(tag, "score", i))
            if i >= 2:
                dve.wait_ge(act_.sem, act_.at(tag, "exp", i - 2))
            if keys == 4:
                nc.vector.scalar_tensor_tensor(score[:, i % 2, 0:S], k.psum[i % 2][:, 0:S], HD ** -0.5,
                                               k.c["window"][:, t * S:(t + 1) * S], ALU.mult,
                                               ALU.add).then_inc(*dve_.did())
            link(nc.vector.tensor_scalar(score[:, i % 2, width - S:width], k.psum[i % 2][:, width - S:width],
                                         HD ** -0.5, None, ALU.mult), tag, "score", i)
            link(nc.vector.tensor_reduce(top[:, t, h:h + 1], score[:, i % 2, :], AX.X, ALU.max))
            link(nc.vector.tensor_scalar(top[:, t, h:h + 1], top[:, t, h:h + 1], sink[:, h:h + 1], -1.0, ALU.max,
                                         ALU.mult), tag, "top", i)
        for t in range(TT):
            link(nc.vector.tensor_tensor(sink_exp[:, t, :], top[:, t, :], sink, ALU.add), tag, "sink", t)
        dve.wait_ge(act_.sem, act_.at(tag, "sink"))
        link(nc.vector.tensor_tensor(den, den, sink_exp, ALU.add))
        link(nc.vector.reciprocal(inv, den))
        dve.wait_ge(pe_.sem, pe_.at(tag, "value", n - 1))
        for t in range(TT):
            link(nc.vector.tensor_tensor(o[:, t, :].rearrange("p (h d) -> p h d", h=NH),
                                         k.psum[4 + t][:, :].rearrange("p (h d) -> p h d", h=NH),
                                         inv[:, t, :].unsqueeze(2).to_broadcast([P, NH, HD]), ALU.mult))
        link(nc.vector.tensor_tensor(sq, o, o, ALU.mult))
        link(nc.vector.tensor_reduce(ssq, sq, AX.X, ALU.add))

    @k.block.scalar
    def _(act):
        for i in range(n + 1):
            if i < n:
                h, t = units[i]
                act.wait_ge(dve_.sem, dve_.at(tag, "top", i))
                if i >= 2:
                    act.wait_ge(pe_.sem, pe_.at(tag, "turned", i - 2))
                nc.scalar.activation(prob[:, i % 2, :], score[:, i % 2, :], ACT.Exp, bias=top[:, t, h:h + 1],
                                     accum_out=den[:, t, h:h + 1]).then_inc(*act_.did(tag, "exp", i))
            u = i - 1
            if u >= 0:
                act.wait_ge(pe_.sem, pe_.at(tag, "turned", u))
                if u >= 2:
                    act.wait_ge(pe_.sem, pe_.at(tag, "value", u - 2))
                nc.scalar.copy(prob_t[:, u % 2, :], k.psum[2 + u % 2][:, 0:width]).then_inc(*act_.did(tag, "prob_t", u))
        act.wait_ge(dve_.sem, dve_.at(tag, "sink", TT - 1))
        nc.scalar.activation(sink_exp, sink_exp, ACT.Exp).then_inc(*act_.did(tag, "sink"))

    inverse_root(k, tag, ssq, 512, EPS, ssq)

    @k.block.vector
    def _(dve):
        dve.wait_ge(act_.sem, act_.at(tag, "root"))
        for t in range(TT):
            nc.vector.tensor_scalar(o[:, t, :], o[:, t, :], ssq[:, t:t + 1], None,
                                    ALU.mult).then_inc(*dve_.did(tag, "normed", t))
    meet(k)
    to_channels(k, tag + " out", o, 4, mix_cm[:, 0:4, cols:cols + S], k.v["g_att"][:, 4 * k.layer:4 * k.layer + 4])
    meet(k)
    k.top = keep


def mlstm(k, tag, z, layer, mix_cm):
    nc, pe_, dve_, act_, pool_ = k.nc, k.pe, k.dve, k.act, k.pool
    W = 2 * S if layer == 0 else S
    TQ = W // P
    rows = 64
    fw, bw = slice(0, 32), slice(32, 64)
    qk = take(k, (P, 4, 2 * S))
    v_one = take(k, (P, 4, 4, P + 1))
    a_col, em_col = take(k, (P, 4, rows)), take(k, (P, 4, rows))
    keep = k.top

    conv_w, conv_b = k.v["conv_w"][:, 20 * layer:20 * layer + 20], k.v["conv_b"][:, 4 * layer:4 * layer + 4]
    conv = take(k, (P, 4, 2 * S))

    @k.block.vector
    def _(dve):
        def seq(ap, lo, hi):
            return ap.rearrange("p (s t) -> p s t", s=2)[:, :, lo:hi]
        for j in range(4):
            nc.vector.tensor_scalar(conv[:, j, :], z[:, 6 + j, :], conv_w[:, 8 + j:9 + j], conv_b[:, j:j + 1],
                                    ALU.mult, ALU.add).then_inc(*dve_.did())
        for tap in (0, 1, 3, 4):
            o = tap - 2
            lo, hi = max(0, -o), min(S, S - o)
            dve.wait_ge(dve_.sem, dve_.count)
            for j in range(4):
                nc.vector.scalar_tensor_tensor(seq(conv[:, j, :], lo, hi), seq(z[:, 6 + j, :], lo + o, hi + o),
                                               conv_w[:, 4 * tap + j:4 * tap + j + 1], seq(conv[:, j, :], lo, hi),
                                               ALU.mult, ALU.add).then_inc(*dve_.did(tag, "conv", tap, j))

    @k.block.tensor
    def _(pe):
        for t in range(4):
            for h in range(4):
                mm = nc.tensor.transpose(k.psum[t][:, h * P:(h + 1) * P], z[:, 10 + h, t * P:(t + 1) * P], k.ident)
            mm.then_inc(*pe_.did(tag, "v", t))

    @k.block.scalar
    def _(act):
        for t in range(4):
            act.wait_ge(pe_.sem, pe_.at(tag, "v", t))
            nc.scalar.copy(v_one[:, t, :, 0:P], k.psum[t][:, :].rearrange("p (h c) -> p h c", h=4)
                           ).then_inc(*act_.did(tag, "v", t))
        act.wait_ge(dve_.sem, dve_.at(tag, "conv", 4, 3))
        nc.scalar.activation(qk, conv, ACT.Silu).then_inc(*act_.did(tag, "qk"))
        nc.scalar.activation(z[:, 14:18, 0:W], z[:, 14:18, 0:W], ACT.Sigmoid).then_inc(*act_.did(tag, "open"))

    @k.block.gpsimd
    def _(pool):
        nc.gpsimd.memset(v_one[:, :, :, P:P + 1], 1.0).then_inc(*pool_.did(tag, "one"))
    meet(k)
    k.top = keep

    gate_i, gate_f, run, best, other = (take(k, (P, 2 * S)) for _ in range(5))
    bias = take(k, (P, 2))
    x_, c_ = slice(0, S), slice(S, 2 * S)

    @k.block.vector
    def _(dve):
        link = linked(dve, dve_)
        v = nc.vector
        link(v.tensor_scalar(bias, k.v["gate_bias"][:, 2 * layer:2 * layer + 2], 1.0 / 15.0, None, ALU.mult),
             tag, "bias")
        dve.wait_ge(act_.sem, act_.at(tag, "forget"))
        link(v.tensor_scalar(gate_i[0:rows], gate_i[0:rows], 15.0, None, ALU.mult))
        link(v.tensor_scalar(gate_f[0:rows], gate_f[0:rows], -1.0, None, ALU.mult))
        link(v.memset(other[0:rows], 1.0))
        for part in (c_, x_):
            link(v.tensor_tensor_scan(run[0:rows, part], other[0:rows, part], gate_f[0:rows, part], 0.0,
                                      ALU.mult, ALU.add))
        end_c, end_x = run[:, 2 * S - 1:2 * S], run[:, S - 1:S]
        link(v.tensor_copy(bias[0:rows, 0:1], end_c[0:rows]))
        link(v.tensor_copy(bias[0:rows, 1:2], end_x[0:rows]))
        link(v.tensor_scalar(run[fw, x_], run[fw, x_], bias[fw, 0:1], None, ALU.add))
        link(v.tensor_tensor(run[bw], gate_f[bw], run[bw], ALU.subtract))
        link(v.tensor_scalar(run[bw, c_], run[bw, c_], bias[bw, 0:1], None, ALU.add))
        link(v.tensor_scalar(run[bw, x_], run[bw, x_], bias[bw, 0:1], bias[bw, 1:2], ALU.add, ALU.add))
        link(v.tensor_tensor(gate_i[0:rows], gate_i[0:rows], run[0:rows], ALU.subtract))
        link(v.tensor_tensor_scan(best[fw, c_], gate_i[fw, c_], gate_i[fw, c_], 0.0, ALU.max, ALU.max))
        link(v.tensor_tensor_scan(best[fw, x_], gate_i[fw, x_], gate_i[fw, x_], best[fw, 2 * S - 1:2 * S],
                                  ALU.max, ALU.max))
        def two(ap, lo, hi):
            return ap[bw].rearrange("p (s t) -> p s t", s=2)[:, :, lo:hi]
        link(v.tensor_scalar(best[bw], gate_i[bw], 0.0, None, ALU.max))
        a, b, shift = best, other, 1
        while shift < S:
            link(v.tensor_tensor(two(b, 0, S - shift), two(a, 0, S - shift), two(a, shift, S), ALU.max))
            link(v.tensor_copy(two(b, S - shift, S), two(a, S - shift, S)))
            a, b, shift = b, a, 2 * shift
        assert a is best
        link(v.tensor_scalar(best[bw, x_], best[bw, x_], best[bw, S:S + 1], None, ALU.max))
        link(v.tensor_tensor(run[0:rows], run[0:rows], best[0:rows], ALU.add), tag, "m")
        link(v.tensor_scalar(best[0:rows], best[0:rows], -1.0, None, ALU.mult), tag, "best")
        for which, out in enumerate((a_col, em_col)):
            dve.wait_ge(pe_.sem, pe_.at(tag, "columns", which))
            link(v.tensor_copy(out, k.psum[which][:, 0:4 * rows].rearrange("p (t r) -> p t r", t=4)))

    @k.block.scalar
    def _(act):
        act.wait_ge(dve_.sem, dve_.at(tag, "bias"))
        nc.scalar.activation(gate_f[0:rows], z[0:rows, 19, :], ACT.Tanh, bias=bias[0:rows, 1:2],
                             scale=1.0 / 15.0).then_inc(*act_.did(tag, "f"))
        nc.scalar.activation(gate_i[0:rows], z[0:rows, 18, :], ACT.Tanh, bias=bias[0:rows, 0:1],
                             scale=1.0 / 15.0).then_inc(*act_.did(tag, "i"))
        act.wait_ge(act_.sem, act_.at(tag, "f"))
        nc.scalar.activation(gate_f[0:rows], gate_f[0:rows], ACT.Exp, scale=-15.0).then_inc(*act_.did(tag, "exp"))
        act.wait_ge(act_.sem, act_.at(tag, "exp"))
        nc.scalar.activation(gate_f[0:rows], gate_f[0:rows], ACT.Ln, bias=1.0).then_inc(*act_.did(tag, "forget"))
        act.wait_ge(dve_.sem, dve_.at(tag, "m"))
        nc.scalar.activation(run[0:rows], run[0:rows], ACT.Exp, scale=-1.0).then_inc(*act_.did(tag, "em"))

    @k.block.tensor
    def _(pe):
        pe.wait_ge(dve_.sem, dve_.at(tag, "m"))
        for which, source in enumerate((gate_i, run)):
            if which == 1:
                pe.wait_ge(act_.sem, act_.at(tag, "em"))
            for t in range(4):
                mm = nc.tensor.transpose(k.psum[which][:, t * rows:(t + 1) * rows], source[0:rows, t * P:(t + 1) * P],
                                         k.ident[0:rows, 0:rows])
            mm.then_inc(*pe_.did(tag, "columns", which))
    meet(k)

    below = best
    h_tm = take(k, (P, TQ, 512))
    expo = take(k, (P, 4, 2 * S))
    den = take(k, (P, 4))
    tri = k.c["tri"].rearrange("p (d t) -> p d t", d=2)
    streams = [(d, h) for d in range(2) for h in range(4)]

    def valid(d, s, t):
        if (s < TT) != (t < TT):
            return t < TT
        return s <= t if d == 0 else s >= t

    def query_width(s):
        return S if s < TT else W

    @k.block.tensor
    def _(pe):
        for n, (d, h) in enumerate(streams):
            r, tile = slice(64 * (h % 2), 64 * (h % 2) + 64), h // 2
            if n:
                pe.wait_ge(dve_.sem, dve_.at(tag, "weight", n - 1, 3))
            nc.tensor.matmul(k.psum[0][:, 0:W], k.c["pick_gate"][0:rows, (4 * d + h) * P:(4 * d + h + 1) * P],
                             below[0:rows, 0:W], start=True, stop=True).then_inc(*pe_.did(tag, "below", n))
            for s in range(4):
                nc.tensor.matmul(k.psum[2 + s][:, 0:query_width(s)], qk[r, 2 + tile, s * P:(s + 1) * P],
                                 qk[r, tile, 0:query_width(s)], start=True,
                                 stop=True).then_inc(*pe_.did(tag, "score", n, s))
            pe.wait_ge(dve_.sem, dve_.at(tag, "masked", n))
            if n:
                pe.wait_ge(dve_.sem, dve_.at(tag, "hidden", n - 1))
            for t in range(TQ):
                keys = [s for s in range(4) if valid(d, s, t)]
                for s in keys:
                    mm = nc.tensor.matmul(k.psum[6 + t // 2][:, (t % 2) * (P + 1):(t % 2 + 1) * (P + 1)],
                                          expo[:, s, t * P:(t + 1) * P], v_one[:, s, h, :],
                                          start=(s == keys[0]), stop=(s == keys[-1]))
            mm.then_inc(*pe_.did(tag, "value", n))

    @k.block.vector
    def _(dve):
        link = linked(dve, dve_)
        v = nc.vector
        for n, (d, h) in enumerate(streams):
            row = 32 * d + h
            dve.wait_ge(pe_.sem, pe_.at(tag, "below", n))
            if n:
                dve.wait_ge(pe_.sem, pe_.at(tag, "value", n - 1))
            for s in range(4):
                w = query_width(s)
                v.tensor_scalar(expo[:, s, 0:w], k.psum[0][:, 0:w], a_col[:, s, row:row + 1], 0.0, ALU.add,
                                ALU.min).then_inc(*dve_.did(tag, "exponent", n, s))
            for s in range(4):
                w = query_width(s)
                dve.wait_ge(act_.sem, act_.at(tag, "exp", n, s))
                dve.wait_ge(pe_.sem, pe_.at(tag, "score", n, s))
                v.scalar_tensor_tensor(expo[:, s, 0:w], k.psum[2 + s][:, 0:w], 0.125, expo[:, s, 0:w], ALU.mult,
                                       ALU.mult).then_inc(*dve_.did(tag, "weight", n, s))
            dve.wait_ge(dve_.sem, dve_.count)
            for s in range(TQ):
                c = slice(s * P, (s + 1) * P)
                v.tensor_tensor(expo[:, s, c], expo[:, s, c], tri[:, d, :],
                                ALU.mult).then_inc(*dve_.did(tag, *(("masked", n) if s == TQ - 1 else ("mask", n, s))))
            dve.wait_ge(pe_.sem, pe_.at(tag, "value", n))
            for pair in range(TQ // 2):
                both = k.psum[6 + pair][:, 0:2 * (P + 1)].rearrange("p (t c) -> p t c", t=2)
                dd = den[:, 2 * pair:2 * pair + 2]
                link(v.tensor_scalar(dd, both[:, :, P], -1.0, None, ALU.mult))
                link(v.tensor_tensor(dd, dd, both[:, :, P], ALU.max))
                link(v.tensor_tensor(dd, dd, em_col[:, 2 * pair:2 * pair + 2, row], ALU.max))
                link(v.reciprocal(dd, dd))
                for j in range(2):
                    out = h_tm[:, 2 * pair + j, h * P:(h + 1) * P]
                    last = 2 * pair + j == TQ - 1
                    name = (tag, "hidden", n) if last else (tag, "hidden part", n, 2 * pair + j)
                    if d == 0:
                        ins = v.tensor_scalar(out, both[:, j, 0:P], dd[:, j:j + 1], None, ALU.mult)
                    else:
                        ins = v.scalar_tensor_tensor(out, both[:, j, 0:P], dd[:, j:j + 1], out, ALU.mult, ALU.add)
                    link(ins, *name)

    @k.block.scalar
    def _(act):
        for n in range(8):
            for s in range(4):
                w = query_width(s)
                act.wait_ge(dve_.sem, dve_.at(tag, "exponent", n, s))
                nc.scalar.activation(expo[:, s, 0:w], expo[:, s, 0:w], ACT.Exp).then_inc(*act_.did(tag, "exp", n, s))
    meet(k)

    sq, ssq = expo.rearrange("p a b -> p (a b)")[:, 0:TQ * 512], a_col.rearrange("p a b -> p (a b)")[:, 0:TQ * 4]
    flat = h_tm.rearrange("p a b -> p (a b)")
    per_head = flat.rearrange("p (n c) -> p n c", c=P)

    @k.block.vector
    def _(dve):
        link = linked(dve, dve_)
        link(nc.vector.tensor_tensor(sq, flat, flat, ALU.mult))
        link(nc.vector.tensor_reduce(ssq, sq.rearrange("p (n c) -> p n c", c=P), AX.X, ALU.add))
    inverse_root(k, tag + " norm", ssq, P, EPS, ssq)

    @k.block.vector
    def _(dve):
        link = linked(dve, dve_)
        dve.wait_ge(act_.sem, act_.at(tag + " norm", "root"))
        link(nc.vector.tensor_tensor(per_head, per_head, ssq.unsqueeze(2).to_broadcast([P, TQ * 4, P]), ALU.mult))
    meet(k)
    to_channels(k, tag + " out", h_tm, 4, mix_cm[:, 4:8, :], k.v["g_ml"][:, 4 * layer:4 * layer + 4], token_tiles=TQ)

    @k.block.vector
    def _(dve):
        dve.wait_ge(dve_.sem, dve_.count)
        nc.vector.tensor_tensor(mix_cm[:, 4:8, 0:W], mix_cm[:, 4:8, 0:W], z[:, 14:18, 0:W],
                                ALU.mult).then_inc(*dve_.did())
    meet(k)


def route(k, xt):
    nc, pe_, dve_, act_ = k.nc, k.pe, k.dve, k.act
    router, bias = take(k, (P, KT, EXPERTS)), take(k, (P, EXPERTS))
    logits, best = take(k, (P, TT, EXPERTS)), take(k, (P, TT, 8))
    at_f, weights, share, tmp = (take(k, (P, TT, 8)) for _ in range(4))
    index = take(k, (P, TT * 8)).bitcast(U32)
    turned = take(k, (P, S))
    loaded = broadcast_row(k, 6, bias)

    @k.block.gpsimd
    def _(pool):
        pool.dma_start(router.rearrange("p a b -> p (a b)"), k.mats[:, 3 * 512:]).then_inc(k.mats_landed, 16)

    @k.block.tensor
    def _(pe):
        pe.wait_ge(k.mats_landed, 32)
        for t in range(TT):
            for kt in range(KT):
                mm = nc.tensor.matmul(k.psum[0][:, t * 8:(t + 1) * 8], xt[:, kt, t * P:(t + 1) * P], router[:, kt, :],
                                      start=(kt == 0), stop=(kt == KT - 1))
        mm.then_inc(*pe_.did("route", "logits"))
        pe.wait_ge(dve_.sem, dve_.at("route", "share"))
        for t in range(TT):
            mm = nc.tensor.transpose(k.psum[1][0:EXPERTS, t * P:(t + 1) * P], share[:, t, :], k.ident)
        mm.then_inc(*pe_.did("route", "turned"))
        pe.wait_ge(dve_.sem, dve_.at("route", "turned"))
        for e in range(EXPERTS):
            mm = nc.tensor.matmul(k.psum[2 + e // 2][:, (e % 2) * S:(e % 2 + 1) * S],
                                  k.c["pick_expert"][0:EXPERTS, e * P:(e + 1) * P], turned[0:EXPERTS, :],
                                  start=True, stop=True)
        mm.then_inc(*pe_.did("route", "spread"))

    @k.block.vector
    def _(dve):
        link = linked(dve, dve_)
        v = nc.vector
        dve.wait_ge(k.row_landed, loaded)
        dve.wait_ge(pe_.sem, pe_.at("route", "logits"))
        link(v.tensor_tensor(logits, k.psum[0][:, 0:TT * 8].rearrange("p (t e) -> p t e", t=TT),
                             bias.unsqueeze(1).to_broadcast([P, TT, EXPERTS]), ALU.add))
        for t in range(TT):
            link(v.max(best[:, t, :], logits[:, t, :]))
            link(v.max_index(index[:, t * 8:(t + 1) * 8], best[:, t, :], logits[:, t, :]))
            link(v.tensor_copy(at_f[:, t, :], index[:, t * 8:(t + 1) * 8]))
        link(v.tensor_tensor(weights[:, :, 1], best[:, :, 1], best[:, :, 0], ALU.subtract), "route", "apart")
        dve.wait_ge(act_.sem, act_.at("route", "exp"))
        link(v.tensor_scalar(weights[:, :, 0], weights[:, :, 1], 1.0, None, ALU.add))
        link(v.reciprocal(weights[:, :, 0], weights[:, :, 0]))
        link(v.tensor_tensor(weights[:, :, 1], weights[:, :, 1], weights[:, :, 0], ALU.mult))
        for t in range(TT):
            for n, out in enumerate((share, tmp)):
                link(v.tensor_scalar(out[:, t, :], k.c["experts"], at_f[:, t, n:n + 1], weights[:, t, n:n + 1],
                                     ALU.is_equal, ALU.mult))
        link(v.tensor_tensor(share, share, tmp, ALU.add), "route", "share")
        dve.wait_ge(pe_.sem, pe_.at("route", "turned"))
        link(v.tensor_copy(turned[0:EXPERTS, :], k.psum[1][0:EXPERTS, 0:S]), "route", "turned")
        dve.wait_ge(pe_.sem, pe_.at("route", "spread"))
        for b in range(4):
            link(v.tensor_copy(k.expert_weight[:, 2 * b * S:2 * (b + 1) * S], k.psum[2 + b][:, :]))

    @k.block.scalar
    def _(act):
        act.wait_ge(dve_.sem, dve_.at("route", "apart"))
        nc.scalar.activation(weights[:, :, 1], weights[:, :, 1], ACT.Exp).then_inc(*act_.did("route", "exp"))
    meet(k)


def final_norm(k):
    nc, dve_, act_ = k.nc, k.dve, k.act
    junk, ssq, gain = take(k, (P, TT, D)), take(k, (P, TT)), take(k, (P, D))
    loaded = broadcast_row(k, ROWS.index("final_g"), gain)

    @k.block.scalar
    def _(act):
        for t in range(TT):
            nc.scalar.activation(junk[:, t, :], k.h[:, t, :], ACT.Square,
                                 accum_out=ssq[:, t:t + 1]).then_inc(*act_.did("final", "ssq", t))

    @k.block.vector
    def _(dve):
        dve.wait_ge(act_.sem, act_.at("final", "ssq", TT - 1))
    inverse_root(k, "final", ssq, D, EPS, ssq)

    @k.block.vector
    def _(dve):
        dve.wait_ge(act_.sem, act_.at("final", "root"))
        dve.wait_ge(k.row_landed, loaded)
        for t in range(TT):
            nc.vector.scalar_tensor_tensor(k.h[:, t, :], k.h[:, t, :], ssq[:, t:t + 1], gain, ALU.mult,
                                           ALU.mult).then_inc(*dve_.did("final", "out", t))
    meet(k)


def block_two(k):
    nc = k.nc
    k.top = 0
    k.ctx = take(k, (P, TT, D))
    sink = take(k, (P, 2, NH))
    k.xt = take(k, (P, KT, 2 * S))
    after_xt = k.top
    k.mix_cm = take(k, (P, KT, 2 * S))
    z_at = k.top
    z = take(k, (P, 20, 2 * S))
    base = k.top

    @k.block.scalar
    def _(act):
        act.dma_start(k.ctx, k.ctx_in.rearrange("(t p) d -> p t d", p=P)).then_inc(k.ctx_landed, 16)
        act.wait_ge(k.ctx_landed, 16)
    for layer in range(2):
        k.layer = layer
        tag = f"layer{layer} "
        sequences = ((0, k.h, 0), (1, k.ctx, S))
        loaded = broadcast_row(k, 4 + layer, sink[:, layer, :])

        @k.block.vector
        def _(dve):
            dve.wait_ge(k.row_landed, loaded)
        k.top = base
        for who, source, cols in sequences:
            k.top = base
            rmsnorm_cm(k, f"{tag}norm1 {who}", source, cols, k.gain[:, layer, 0, who, :], k.mod[:, layer, who, 0:KT])
            meet(k)
        if layer == 0:
            widths = [2 * S] * 20
        else:
            widths = [S] * 4 + [2 * S] * 2 + [S] * 2 + [2 * S] * 6 + [S] * 4 + [2 * S] * 2
        if layer == 1:
            @k.block.gpsimd
            def _(pool):
                nc.gpsimd.memset(z[:, 6:8, S:2 * S], 0.0).then_inc(*k.pool.did())
        k.top = base
        project(k, tag + "w_in", 0, widths, z, after_xt)
        meet(k)
        k.top = base
        rope(k, tag + "rope", z, 5, k.c["rope2_swap"], k.c["rope2_cos"], k.c["rope2_sin"])
        meet(k)
        k.top = base
        v_tm = take(k, (P, 4, P))
        to_tokens(k, tag + "v", z[:, 5:6, :], 1, v_tm, token_tiles=4)
        meet(k)
        for who, _, cols in sequences[:2 - layer]:
            sink_attention(k, f"{tag}attention {who}", z, cols, 4 - 2 * who, v_tm, sink[:, layer, :], k.mix_cm)
        k.top = base
        mlstm(k, tag + "mlstm", z, layer, k.mix_cm)
        gates = []
        k.top = base
        for who, _, _ in sequences[:2 - layer]:
            row = take(k, (P, D))
            gates.append(row)
            keep = k.top
            gate_rows(k, f"{tag}gate1 {who}", who, 16, row)
            meet(k)
            k.top = keep
        keep = k.top
        mix_down(k, tag + "w_out", k.mix_cm, z_at, token_tiles=TT * (2 - layer))
        meet(k)
        k.top = keep
        for who, target, _ in sequences[:2 - layer]:
            gated_add(k, f"{tag}mix {who}", 4 * who, gates[who], target)
        meet(k)
        for who, target, cols in sequences[:2 - layer]:
            k.top = after_xt
            gate = take(k, (P, D))
            keep = k.top
            gate_rows(k, f"{tag}gate2 {who}", who, 40, gate)
            meet(k)
            k.top = keep
            rmsnorm_cm(k, f"{tag}norm2 {who}", target, cols, k.gain[:, layer, 1, who, :], k.mod[:, layer, who, 24:24 + KT])
            meet(k)
            k.top = keep
            if layer == 0:
                ffn(k, f"{tag}ffn {who}", cols, 5, 2)
            else:
                k.expert_weight = take(k, (P, EXPERTS * S))
                route(k, k.xt)
                ffn(k, tag + "experts", 0, EXPERTS // 2 * (FT // 2), 0, experts=True)
            meet(k)
            k.top = keep
            gated_add(k, f"{tag}ffn add {who}", 0, gate, target)
            meet(k)
    k.top = after_xt
    final_norm(k)



def column_chunks(w):
    n = w.shape[1] // P
    return w.reshape(KT, P, n, P).transpose(2, 1, 0, 3).reshape(n, P, CW)


def half_chunks(w):
    return w.reshape(4, 2, P, 2, 512).transpose(3, 0, 2, 1, 4).reshape(8, P, CW)


def round_chunks(parts, tiles):
    return np.stack([parts[j][("gate", "up", "down").index(what)] for what, j in round_steps(tiles)])


def swiglu_parts(w_gate, w_up, w_down):
    return np.stack([column_chunks(w_gate), column_chunks(w_up), w_down.reshape(FT, P, D)], 1)


def dense_chunks(w_gate, w_up, w_down):
    parts = swiglu_parts(w_gate, w_up, w_down)
    return np.concatenate([round_chunks(parts[at:at + 4], min(4, FT - at)) for at in range(0, FT, 4)])


def by_channel(v):
    return np.asarray(v).reshape(-1, P).T


def constants():
    cols, n = constant_columns()
    out = np.zeros((P, n), np.float32)

    def put(name, value):
        o, w = cols[name]
        value = np.asarray(value, np.float32)
        out[:value.shape[0], o:o + w] = value.reshape(value.shape[0], w)

    i = np.arange(P)
    put("ident", np.eye(P))
    put("ones", np.ones((P, P)))

    def swap(half):
        m = np.zeros((P, P))
        for c in range(P):
            if c % (2 * half) < half:
                m[c + half, c] = -1.0
            else:
                m[c - half, c] = 1.0
        return m
    put("rope1_swap", swap(32))
    put("rope2_swap", swap(16))
    put("head_ones", i[:, None] // HD == i[None, :] // HD)
    token = np.arange(S, dtype=np.float32)
    inv = (10000.0 ** (-np.arange(0, HD, 2, dtype=np.float32) / HD)).astype(np.float32)
    angle = (token[None, :] * inv[i % 32][:, None]).astype(np.float32)
    put("rope1_cos", np.cos(angle))
    put("rope1_sin", np.sin(angle))
    inv = (10000.0 ** (-np.arange(16, dtype=np.float32) / 16)).astype(np.float32)
    where = np.where(((i % HD) < 32)[:, None], token[None, :] // 64, token[None, :] % 64).astype(np.float32)
    angle = (where * inv[i % 16][:, None]).astype(np.float32)
    put("rope2_cos", np.cos(angle))
    put("rope2_sin", np.sin(angle))
    q = (np.arange(TT)[None, :, None] * P + i[:, None, None])
    key = np.arange(S)[None, None, :]
    apart = np.abs(q - key)
    count = (apart <= 64) * 1 + (apart % 4 == 0) * 1 + (apart % 16 == 0) * 1
    put("dilated", np.where(count > 0, np.log(np.maximum(count, 1)), NEG))
    put("window", np.where(apart <= 128, 0.0, NEG))
    put("chunk_keep", np.broadcast_to(token[None, :] % CH != 0, (P, S)))
    row, col = (i % CH)[:, None], np.arange(CH)[None, :]
    masks = []
    for parity in range(2):
        forward = ((i // CH) == parity)[:, None]
        before = np.where(forward, row < col, row > col)
        upto = before | (row == col)
        after = np.where(forward, row > col, row < col)
        block = (row // 16) == (col // 16)
        masks.append([-1.0 * (before & block), -1.0 * (before & ~block), -1.0 * (after & block), before, upto])
    put("chunk_eye", row == col)
    put("rwkv_masks", np.asarray(masks, np.float32).transpose(2, 0, 1, 3))
    put("tri", np.stack([i[:, None] <= i[None, :], i[:, None] >= i[None, :]], 1))
    pick = np.zeros((P, 8, P))
    for r in range(8):
        pick[(r // 4) * 32 + r % 4, r, :] = 1.0
    put("pick_gate", pick)
    pick = np.zeros((P, 8, P))
    for r in range(8):
        pick[r, r, :] = 1.0
    put("pick_expert", pick)
    put("experts", np.broadcast_to(np.arange(EXPERTS)[None, :], (P, EXPERTS)))
    put("pair_mask", i[:, None] // HD == i[None, :] // HD)
    return out


def pack_vectors(v):
    cols, n = vector_columns()
    out = np.zeros((P, n), np.float32)

    def put(name, value):
        o, w = cols[name]
        assert value.shape == (P, w), (name, value.shape)
        out[:, o:o + w] = value
    put("ffn1_pre_g", by_channel(v["ffn1_pre_g"]))
    put("mix_pre_g", by_channel(v["mix_pre_g"]))
    put("mu_prev", by_channel(v["rwkv_mu_prev"]))
    put("mu_next", by_channel(v["rwkv_mu_next"]))
    put("w0", by_channel(v["rwkv_w0"]))
    put("a0", by_channel(v["rwkv_a0"]))
    for name in ("k_k", "k_a", "r_k", "lnx_w", "lnx_b"):
        put(name, by_channel(v["rwkv_" + name]))
    put("attn_out_g", by_channel(v["attn_out_g"]))
    put("ffn2_pre_g", by_channel(v["ffn2_pre_g"]))
    put("norm1_g", by_channel(v["norm1_g_2"]))
    put("norm2_g", by_channel(v["norm2_g_2"]))
    put("b_mod", by_channel(v["b_mod_2"]))
    put("conv_w", by_channel(v["conv_w_2"]))
    put("conv_b", by_channel(v["conv_b_2"]))
    bias = np.zeros((P, 2, 2), np.float32)
    g = v["b_gates_2"].reshape(2, 2, 2, 4)
    for d in range(2):
        bias[32 * d:32 * d + 4] = g[:, d].transpose(2, 0, 1)
    put("gate_bias", bias.reshape(P, 4))
    put("g_att", by_channel(v["g_att_2"]))
    put("g_ml", by_channel(v["g_ml_2"]))
    put("cond", np.stack([by_channel(v["c_2"]), by_channel(v["c_ctx_2"])], 2).reshape(P, 2 * KT))
    return out


def w_in_2_columns(w):
    q = w[:, :512].reshape(D, 2, 4, HD).transpose(0, 2, 1, 3).reshape(D, 512)
    gates = w[:, 2304:].reshape(D, 2, 2, 4)
    rows = np.zeros((D, 2, P), np.float32)
    for d in range(2):
        rows[:, :, 32 * d:32 * d + 4] = gates[:, d]
    return np.concatenate([q, w[:, 512:2304], rows.reshape(D, 2 * P)], 1)


def chunk_stream(v):
    parts = [
        dense_chunks(v["ffn1_w_gate"][0], v["ffn1_w_up"][0], v["ffn1_w_down"][0]),
        column_chunks(v["w_in"][0]), column_chunks(v["w_mod_2"][0]), column_chunks(v["w_mod_2"][1]),
        half_chunks(v["w_out"][0]),
        dense_chunks(v["ffn2_w_gate"][0], v["ffn2_w_up"][0], v["ffn2_w_down"][0]),
    ]
    for layer in range(2):
        parts += [column_chunks(w_in_2_columns(v["w_in_2"][layer])), half_chunks(v["w_out_2"][layer])]
        if layer == 0:
            dense = dense_chunks(v["ffn_w1_2"][0], v["ffn_w3_2"][0], v["ffn_w2_2"][0])
            parts += [dense, dense]
    for couple in range(0, EXPERTS, 2):
        a, b = (swiglu_parts(v["exp_w1_2"][0, e], v["exp_w3_2"][0, e], v["exp_w2_2"][0, e])
                for e in (couple, couple + 1))
        parts += [round_chunks(np.concatenate([a[at:at + 2], b[at:at + 2]]), 4) for at in range(0, FT, 2)]
    return np.concatenate(parts)


def pack_matrices(v):
    router = v["w_router_2"][0].reshape(KT, P, EXPERTS).transpose(1, 0, 2).reshape(P, KT * EXPERTS)
    return np.concatenate([v["rwkv_w2"][0].reshape(P, 512), v["rwkv_a2"][0].reshape(P, 512), v["rwkv_g2"][0],
                           router], 1)


def pack_rows(v):
    out = np.zeros((7, D), np.float32)
    for n, name in enumerate(("ffn1_post_g", "mix_post_g", "ffn2_post_g", "final_g_2")):
        out[n] = v[name].reshape(-1)
    out[4:6, :NH] = v["attn_sink_2"]
    out[6, :EXPERTS] = v["b_router_2"][0]
    return out



def kernel(**inputs):
    import concourse.bacc as bacc
    from concourse.bass_utils import run_bass_kernel_spmd

    v = {name: np.asarray(a) for name, a in inputs.items()}
    arrays = {
        "in_x": np.ascontiguousarray(v["x"][0]), "in_ctx": np.ascontiguousarray(v["ctx_2"][0]),
        "in_stream": chunk_stream(v), "in_constants": constants(), "in_vectors": pack_vectors(v),
        "in_matrices": pack_matrices(v), "in_rows": pack_rows(v),
    }
    table = {}
    for _ in range(2):
        nc = bacc.Bacc("TRN2", target_bir_lowering=False, num_devices=1)
        a = {name[3:]: nc.dram_tensor(name, x.shape, F32, kind="ExternalInput").ap() for name, x in arrays.items()}
        a["out"] = nc.dram_tensor("out_h", (S, D), F32, kind="ExternalOutput").ap()
        build(nc, a, table, len(arrays["in_stream"]))
        assert table["chunks"] == len(arrays["in_stream"])
        table["complete"] = True
    result = run_bass_kernel_spmd(nc, [arrays], core_ids=[0])
    return result.results[0]["out_h"].reshape(1, S, D)
```
